# Optimizing a Trainium2 kernel written in Bass

```python
import jax, jax.numpy as jnp
from jax import lax
import numpy as np

D_MODEL = 1024
BATCH = 1
SEQ = 2048
DEPTH = 1
DEC_BATCH = 8
DEC_SEQ = 16
PAST_LEN = 128

CHUNK = 64
D_CONV = 512
CONV_WIDTH = 31
D_SG = 512
SG_HEADS = 4
SG_HEAD_DIM = D_SG // SG_HEADS
SG_CHUNK = 128
D_MIX = D_CONV + D_SG
N_MEM = 256
X_HEADS = 4
X_HEAD_DIM = D_MODEL // X_HEADS
N_GROUPS = 4
EXPERTS_PER_GROUP = 8
N_EXPERTS = N_GROUPS * EXPERTS_PER_GROUP
TOP_K = 2
D_EXPERT = 512
MOE_BLOCK = 128
EPS = 1e-6

kernel_name = "hybrid_conv_sgmlp_memxattn_hmoe_stream_step"

def rms_norm(x, g):
    xf = x.astype(jnp.float32)
    y = xf * lax.rsqrt(jnp.mean(xf * xf, axis=-1, keepdims=True) + EPS)
    return (y * g.astype(jnp.float32)).astype(x.dtype)

def layer_norm(x, g, b):
    xf = x.astype(jnp.float32)
    mu = jnp.mean(xf, axis=-1, keepdims=True)
    var = jnp.mean(jnp.square(xf - mu), axis=-1, keepdims=True)
    y = (xf - mu) * lax.rsqrt(var + EPS) * g.astype(jnp.float32) + b.astype(jnp.float32)
    return y.astype(x.dtype)

def conformer_conv(a_in, a_gate, hist, conv_w, conv_b, ln_g, ln_b):
    a = a_in * jax.nn.sigmoid(a_gate)
    ext = jnp.concatenate([hist.astype(a.dtype), a], axis=1)
    y = lax.conv_general_dilated(
        ext, conv_w[:, None, :].astype(ext.dtype), window_strides=(1,), padding='VALID',
        dimension_numbers=('NWC', 'WIO', 'NWC'), feature_group_count=D_CONV)
    y = jax.nn.silu(layer_norm(y + conv_b.astype(y.dtype), ln_g, ln_b))
    return y, ext[:, -(CONV_WIDTH - 1):]

def spatial_gate(u, v, w_s, b_s):
    B, T, _ = v.shape
    L = min(T, SG_CHUNK)
    mask = jnp.tril(jnp.ones((L, L), dtype=bool))
    w = jnp.where(mask, w_s[:, :L, :L], 0).astype(v.dtype)
    vc = v.reshape(B, T // L, L, SG_HEADS, SG_HEAD_DIM)
    s = jnp.einsum('hij,bcjhd->bcihd', w, vc) + b_s[:, :L].T[:, :, None].astype(v.dtype)
    return u * s.reshape(B, T, D_SG)

def memory_kv(mem, g_mem, w_mk, w_mv):
    B = mem.shape[0]
    m = rms_norm(mem, g_mem)
    k = (m @ w_mk).reshape(B, N_MEM, X_HEADS, X_HEAD_DIM)
    v = (m @ w_mv).reshape(B, N_MEM, X_HEADS, X_HEAD_DIM)
    return k, v

def memory_attend(h, mem_k, mem_v, w_xq, w_xo):
    B, T, _ = h.shape
    q = (h @ w_xq).reshape(B, T, X_HEADS, X_HEAD_DIM)
    s = jnp.einsum('bqhd,bkhd->bhqk', q, mem_k.astype(q.dtype)).astype(jnp.float32) * (X_HEAD_DIM ** -0.5)
    p = jax.nn.softmax(s, axis=-1).astype(q.dtype)
    o = jnp.einsum('bhqk,bkhd->bqhd', p, mem_v.astype(q.dtype)).reshape(B, T, D_MODEL)
    return o @ w_xo

def routed_experts(t, expert, w_eg, w_eu, w_ed):
    n, D = t.shape
    a = n * TOP_K
    flat = expert.reshape(-1)
    order = jnp.argsort(flat)
    sorted_e = flat[order]
    counts = jnp.bincount(flat, length=N_EXPERTS)
    padded = (counts + MOE_BLOCK - 1) // MOE_BLOCK * MOE_BLOCK
    pad_end = jnp.cumsum(padded)
    pad_start = pad_end - padded
    start = jnp.cumsum(counts) - counts
    slot = pad_start[sorted_e] + jnp.arange(a, dtype=jnp.int32) - start[sorted_e]
    n_blocks = -(-a // MOE_BLOCK) + N_EXPERTS
    token_of_slot = jnp.full((n_blocks * MOE_BLOCK,), n, jnp.int32).at[slot].set((order // TOP_K).astype(jnp.int32))
    block_expert = jnp.minimum(
        jnp.searchsorted(pad_end, jnp.arange(n_blocks, dtype=jnp.int32) * MOE_BLOCK, side='right'), N_EXPERTS - 1)
    xs = jnp.concatenate([t, jnp.zeros((1, D), t.dtype)], axis=0)[token_of_slot].reshape(n_blocks, MOE_BLOCK, D)

    def expert_block(args):
        xb, e = args
        return (jax.nn.silu(xb @ w_eg[e]) * (xb @ w_eu[e])) @ w_ed[e]

    ys = lax.map(expert_block, (xs, block_expert)).reshape(-1, D)
    slot_of_assign = jnp.zeros((a,), jnp.int32).at[order].set(slot)
    return ys[slot_of_assign].reshape(n, TOP_K, D)

def hier_moe(h, w_rg, b_rg, w_re, b_re, w_eg, w_eu, w_ed):
    B, T, D = h.shape
    t = h.reshape(-1, D)
    lg = (t @ w_rg).astype(jnp.float32) + b_rg.astype(jnp.float32)
    p_g = jax.nn.softmax(lg, axis=-1)
    g_idx = jnp.argmax(lg, axis=-1)
    g_w = jnp.take_along_axis(p_g, g_idx[:, None], axis=1)
    le = jnp.einsum('nd,gde->nge', t, w_re).astype(jnp.float32) + b_re.astype(jnp.float32)
    le = jnp.take_along_axis(le, g_idx[:, None, None], axis=1)[:, 0]
    top_v, top_i = lax.top_k(le, TOP_K)
    gate = g_w * jax.nn.softmax(top_v, axis=-1)
    expert = (g_idx[:, None] * EXPERTS_PER_GROUP + top_i).astype(jnp.int32)
    y = routed_experts(t, expert, w_eg, w_eu, w_ed)
    return jnp.einsum('nk,nkd->nd', gate.astype(t.dtype), y).reshape(B, T, D)

def trunk_layer(x, conv_hist, mem_k, mem_v, g_mix, w_in, conv_w, conv_b, ln_conv_g, ln_conv_b, ln_v_g, ln_v_b,
                w_sg, b_sg, w_out, g_xattn, w_xq, w_xo, g_ffn, w_rg, b_rg, w_re, b_re, w_eg, w_eu, w_ed):
    h = rms_norm(x, g_mix)
    z = h @ w_in
    a_in, a_gate, u, v = jnp.split(z, [D_CONV, 2 * D_CONV, 2 * D_CONV + D_SG], axis=-1)
    a_out, new_hist = conformer_conv(a_in, a_gate, conv_hist, conv_w, conv_b, ln_conv_g, ln_conv_b)
    v = layer_norm(v, ln_v_g, ln_v_b)
    b_out = spatial_gate(u, v, w_sg, b_sg)
    x = x + jnp.concatenate([a_out, b_out], axis=-1) @ w_out
    x = x + memory_attend(rms_norm(x, g_xattn), mem_k, mem_v, w_xq, w_xo)
    x = x + hier_moe(rms_norm(x, g_ffn), w_rg, b_rg, w_re, b_re, w_eg, w_eu, w_ed)
    return x, new_hist, v

def setup_inputs(seed: int = 0) -> dict:
    key = jax.random.key(seed)
    ks = iter(jax.random.split(key, 40))

    def nrm(shape, scale):
        return jax.random.normal(next(ks), shape, jnp.float32) * scale

    def gain(shape):
        return 1.0 + nrm(shape, 0.02)

    return {
        "x_prompt": nrm((BATCH, SEQ, D_MODEL), 1.0),
        "x_sample": nrm((DEC_BATCH, DEC_SEQ, D_MODEL), 1.0),
        "mem_prompt": nrm((BATCH, N_MEM, D_MODEL), 1.0),
        "state_conv": nrm((DEPTH, DEC_BATCH, CONV_WIDTH - 1, D_CONV), 0.5),
        "cache_mem_k": nrm((DEPTH, DEC_BATCH, N_MEM, X_HEADS, X_HEAD_DIM), 1.0),
        "cache_mem_v": nrm((DEPTH, DEC_BATCH, N_MEM, X_HEADS, X_HEAD_DIM), 1.0),
        "g_mix": gain((DEPTH, D_MODEL)),
        "w_in": nrm((DEPTH, D_MODEL, 2 * D_CONV + 2 * D_SG), D_MODEL ** -0.5),
        "conv_w": nrm((DEPTH, CONV_WIDTH, D_CONV), CONV_WIDTH ** -0.5),
        "conv_b": nrm((DEPTH, D_CONV), 0.02),
        "ln_conv_g": gain((DEPTH, D_CONV)),
        "ln_conv_b": nrm((DEPTH, D_CONV), 0.02),
        "ln_v_g": gain((DEPTH, D_SG)),
        "ln_v_b": nrm((DEPTH, D_SG), 0.02),
        "w_sg": nrm((DEPTH, SG_HEADS, SG_CHUNK, SG_CHUNK), SG_CHUNK ** -0.5),
        "b_sg": 1.0 + nrm((DEPTH, SG_HEADS, SG_CHUNK), 0.1),
        "w_out": nrm((DEPTH, D_MIX, D_MODEL), D_MIX ** -0.5),
        "g_mem": gain((DEPTH, D_MODEL)),
        "w_mk": nrm((DEPTH, D_MODEL, D_MODEL), D_MODEL ** -0.5),
        "w_mv": nrm((DEPTH, D_MODEL, D_MODEL), D_MODEL ** -0.5),
        "g_xattn": gain((DEPTH, D_MODEL)),
        "w_xq": nrm((DEPTH, D_MODEL, D_MODEL), D_MODEL ** -0.5),
        "w_xo": nrm((DEPTH, D_MODEL, D_MODEL), D_MODEL ** -0.5),
        "g_ffn": gain((DEPTH, D_MODEL)),
        "w_router_group": nrm((DEPTH, D_MODEL, N_GROUPS), D_MODEL ** -0.5),
        "b_router_group": nrm((DEPTH, N_GROUPS), 0.01),
        "w_router_expert": nrm((DEPTH, N_GROUPS, D_MODEL, EXPERTS_PER_GROUP), D_MODEL ** -0.5),
        "b_router_expert": nrm((DEPTH, N_GROUPS, EXPERTS_PER_GROUP), 0.01),
        "w_expert_gate": nrm((DEPTH, N_EXPERTS, D_MODEL, D_EXPERT), D_MODEL ** -0.5),
        "w_expert_up": nrm((DEPTH, N_EXPERTS, D_MODEL, D_EXPERT), D_MODEL ** -0.5),
        "w_expert_down": nrm((DEPTH, N_EXPERTS, D_EXPERT, D_MODEL), D_EXPERT ** -0.5),
        "g_final": gain((D_MODEL,)),
    }

def reference(x_prompt, x_sample, mem_prompt, state_conv, cache_mem_k, cache_mem_v, g_mix, w_in, conv_w, conv_b,
              ln_conv_g, ln_conv_b, ln_v_g, ln_v_b, w_sg, b_sg, w_out, g_mem, w_mk, w_mv, g_xattn, w_xq, w_xo,
              g_ffn, w_router_group, b_router_group, w_router_expert, b_router_expert, w_expert_gate,
              w_expert_up, w_expert_down, g_final):
    xp = x_prompt
    xs = x_sample
    conv_p, conv_s, mk_p, mv_p, sgv_s = [], [], [], [], []
    for i in range(DEPTH):
        lw = (g_mix[i], w_in[i], conv_w[i], conv_b[i], ln_conv_g[i], ln_conv_b[i], ln_v_g[i], ln_v_b[i],
              w_sg[i], b_sg[i], w_out[i], g_xattn[i], w_xq[i], w_xo[i], g_ffn[i], w_router_group[i],
              b_router_group[i], w_router_expert[i], b_router_expert[i], w_expert_gate[i], w_expert_up[i],
              w_expert_down[i])
        k_p, v_p = memory_kv(mem_prompt, g_mem[i], w_mk[i], w_mv[i])
        hist0 = jnp.zeros((xp.shape[0], CONV_WIDTH - 1, D_CONV), xp.dtype)
        xp, hist_p, _ = trunk_layer(xp, hist0, k_p, v_p, *lw)
        xs, hist_s, v_s = trunk_layer(xs, state_conv[i], cache_mem_k[i], cache_mem_v[i], *lw)
        conv_p.append(hist_p)
        conv_s.append(hist_s)
        mk_p.append(k_p)
        mv_p.append(v_p)
        sgv_s.append(v_s)
    y_prompt = rms_norm(xp, g_final)
    y_sample = rms_norm(xs, g_final)
    new_state_conv_prompt = jnp.stack(conv_p)
    new_state_conv_sample = jnp.stack(conv_s)
    new_cache_mem_k_prompt = jnp.stack(mk_p)
    new_cache_mem_v_prompt = jnp.stack(mv_p)
    new_state_sg_v_sample = jnp.stack(sgv_s)
    return (y_prompt, y_sample, new_state_conv_prompt, new_state_conv_sample, new_cache_mem_k_prompt,
            new_cache_mem_v_prompt, new_state_sg_v_sample)


_drawn_inputs = setup_inputs


def setup_inputs(seed=0):
    import zlib

    import numpy as np

    out = dict(_drawn_inputs(seed))
    spreads = {}
    factors = {'conv_b': 2.861,
     'ln_conv_g': 3.999,
     'ln_conv_b': 2.869,
     'ln_v_g': 2.89,
     'ln_v_b': 2.861,
     'g_mem': 2.876,
     'g_xattn': 8.0,
     'g_ffn': 2.717,
     'b_router_group': 5.112,
     'b_router_expert': 5.61,
     'g_final': 2.9}
    for name, (base, spread) in spreads.items():
        noise = np.random.default_rng([zlib.crc32(name.encode()), seed]).standard_normal(out[name].shape)
        drawn = base * np.exp(spread * noise) if base else spread * noise
        out[name] = __import__('jax').numpy.asarray(drawn.astype(out[name].dtype))
    for name, factor in factors.items():
        out[name] = (out[name] * factor).astype(out[name].dtype)
    return out
```

```python
from contextlib import ExitStack, contextmanager

import numpy as np
import concourse.bass as bass
from concourse import mybir

F32 = mybir.dt.float32
I32 = mybir.dt.int32
U32 = mybir.dt.uint32
ALU = mybir.AluOpType
ACT = mybir.ActivationFunctionType
X = mybir.AxisListType.X

P = 128
D = 1024
KD = D // P
NT = 17
PT = 16
SEQS, SLEN = 8, 16
DC = 512
CG = DC // P
TAPS = 31
HIST = TAPS - 1
HEADS, HD = 4, 256
NMEM = 256
SCALE = HD ** -0.5
NG, EPG, NE = 4, 8, 32
DE = 512
KE = DE // P
TOK = NT * P
PAIRS = 2 * TOK
CAP = TOK
NBMAX = (PAIRS - NE) // P + NE
EXPERT_COLS = 3 * 4096
EPS = 1e-6
LOW = -3.0e38


class Tile:

    def __init__(self, v, half, par):
        self.v, self.half, self.par = v, half, par

    def at(self, k):
        par = (self.par + k) % 2
        return Tile(self.v + k, self.half + (self.par + k - par) // 2, par)

    def exists(self, n=NT):
        return not isinstance(self.v, int) or 0 <= self.v < n


def fixed(v):
    return Tile(v, v // 2, v % 2)


def need(eng, sem, value):
    if isinstance(value, int) and value <= 0:
        return
    eng.wait_ge(sem, value)


def steps(eng, step, first, pairs, total):
    for s in range(first):
        step(fixed(s))
    if pairs:
        with eng.Fori(0, pairs) as g:
            for u in range(2):
                step(Tile(2 * g + (first + u), g + first // 2, u))
    for s in range(first + 2 * pairs, total):
        step(fixed(s))


def build(nc, I, O):
    top = ExitStack()
    stages, stage_sems = [], []

    @contextmanager
    def one_stage():
        with ExitStack() as st:
            stages.append(st)
            yield st
            for handle in stage_sems:
                nc.gpsimd.sem_clear(handle)
            stage_sems.clear()
            nc.all_engine_barrier()

    with top:
        def alloc(stack):
            def sb(name, shape, dt=F32):
                return stack.enter_context(nc.sbuf_tensor(name, shape, dt))

            def pb(name, shape, dt=F32):
                return stack.enter_context(nc.psum_tensor(name, shape, dt))

            def sem(name):
                handle = stack.enter_context(nc.semaphore(name))
                if stack in stages:
                    stage_sems.append(handle)
                return handle
            return sb, pb, sem

        sb, _, sem = alloc(top)
        mixa_d = nc.dram_tensor("mixa_scratch", [NT, P, DC], F32, kind="Internal").ap()
        mixb_d = nc.dram_tensor("mixb_scratch", [NT, P, DC], F32, kind="Internal").ap()
        x1_d = nc.dram_tensor("x1_scratch", [NT, P, D], F32, kind="Internal").ap()
        oT_d = nc.dram_tensor("oT_scratch", [NT, P, D], F32, kind="Internal").ap()
        x2_d = nc.dram_tensor("x2_scratch", [NT, P, D], F32, kind="Internal").ap()
        h3_d = nc.dram_tensor("h3_scratch", [TOK + P // 2, D], F32, kind="Internal").ap()
        y_d = nc.dram_tensor("y_scratch", [PAIRS + P, D], F32, kind="Internal").ap()
        table_d = nc.dram_tensor("table_scratch", [NE * CAP, 1], I32, kind="Internal").ap()

        ident = sb("ident", [P, P])
        ones = sb("ones", [P, P])
        lower = sb("lower", [P, P])
        mhalf = sb("mhalf", [P, 1])
        gcol = sb("gcol", [P, 3 * KD])
        pcol = sb("pcol", [P, CG, 34])
        gates = sb("gates", [P, NT, 2])
        total = sb("total", [P, NE])
        W = sb("W", [P, 32768])
        w_in = W[:, 0:16384].rearrange("p (k n) -> p k n", k=KD)
        w_out = W[:, 16384:24576].rearrange("p (k n) -> p k n", k=KD)
        w_xq = W[:, 24576:32768].rearrange("p (k n) -> p k n", k=KD)
        w_xo = W[:, 0:8192].rearrange("p (k n) -> p k n", k=KD)
        w_mk = W[:, 16384:24576].rearrange("p (k n) -> p k n", k=KD)
        w_mv = W[:, 24576:32768].rearrange("p (k n) -> p k n", k=KD)
        experts = W[:, 8192:32768]
        settled = {nc.vector: sem("settled_vector"), nc.gpsimd: sem("settled_pool")}

        def settle(eng):
            eng.sem_inc(settled[eng], 1)

        win_here = sem("win_here")
        wout_here = sem("wout_here")
        wxq_here = sem("wxq_here")
        wxo_here = sem("wxo_here")
        kv_stack = ExitStack()
        sbk, _, _ = alloc(kv_stack)
        KT = sbk("KT", [P, 8, NMEM])
        V = sbk("V", [P, 2, D])
        mix_stack = ExitStack()
        sbm, _, _ = alloc(mix_stack)
        sgT = sbm("sgT", [P, HEADS, P])
        sgT_s = sbm("sgT_s", [P, HEADS, P])
        bsg = sbm("bsg", [P, HEADS])
        bsg_s = sbm("bsg_s", [P, HEADS])
        sext = sbm("sext", [P, CG, SEQS, HIST + SLEN])

        x_p = I["x_prompt"].rearrange("b (t p) d -> (b t) p d", p=P)
        x_s = I["x_sample"].rearrange("b t d -> (b t) d")
        kview = "(k p) n -> p k n"

        def load_x(sp, dst, t):
            if isinstance(t.v, int) and t.v == PT:
                return sp.dma_start(dst, x_s)
            return sp.dma_start(dst, x_p[bass.ds(t.v, 1), :, :].rearrange("a p d -> (a p) d"))

        def row(dram, t):
            return dram[bass.ds(t.v, 1), :, :].rearrange("a p d -> (a p) d")

        with one_stage() as st:
            sb, pb, sem = alloc(st)
            mem = sb("mem", [P, 2, D])
            memn = sb("memn", [P, D])
            memT = sb("memT", [P, KD, NMEM])
            junk = memn
            K = mem
            ss = sb("m_ss", [P, 2])
            rstd = sb("m_rstd", [P, 2])
            prow = memT[0:34, 0:2, :].rearrange("p a b -> p (a b)")
            sgw = sb("sgw", [P, HEADS, P])
            sgw_s = sb("sgw_s", [P, HEADS, P])
            tmp = [sb(f"m_tmp{i}", [P, DC]) for i in range(1)]
            grow = sb("grow", [3 * KD, P])
            prow = sb("prow", [34, DC])
            hrow = sb("hrow", [120, 2, DC])
            pst = [pb(f"m_pst{i}", [P, 8, P]) for i in range(1)]
            psc = [pb(f"m_psc{i}", [P, 4, P]) for i in range(2)]
            psk = [pb(f"m_psk{i}", [P, 512]) for i in range(4)]
            mem_here = sem("mem_here")
            small_here = sem("small_here")
            sg_here = sem("sg_here")
            blocks_here = sem("blocks_here")
            wmk_here = sem("wmk_here")
            wmv_here = sem("wmv_here")
            ident_set = sem("ident_set")
            ident_done = sem("ident_done")
            sgs_zero = sem("sgs_zero")
            sg_masked = sem("sg_masked")
            squares = sem("m_squares")
            eps_added = sem("m_eps")
            rstd_done = sem("m_rstd_done")
            normed = sem("m_normed")
            turned = sem("m_turned")
            memT_done = sem("memT_done")
            kv_psum = sem("kv_psum")
            kv_sbuf = sem("kv_sbuf")
            kt_psum = sem("kt_psum")
            kt_done = sem("kt_done")
            kv_out = sem("kv_out")
            const_psum = sem("const_psum")
            const_done = sem("const_done")
            table_set = sem("table_set")
            table_sent = sem("table_sent")
            hist_out = sem("hist_out")
            tabf = sb("tabf", [P, NE * CAP // P], I32)
            tabm = sb("tabm", [P, NE * CAP // P], I32)
            zrow = sb("zrow", [P // 2, D])
            with nc.Block() as block:
                @block.sync
                def _(sp):
                    sp.dma_start(mem[:], I["mem_prompt"].rearrange("b (m p) d -> p (b m) d", p=P)).then_inc(mem_here, 16)
                    sp.dma_start(w_mk, I["w_mk"][0].rearrange(kview, p=P)).then_inc(wmk_here, 16)
                    sp.dma_start(w_mv, I["w_mv"][0].rearrange(kview, p=P)).then_inc(wmv_here, 16)
                    for n in range(4):
                        sp.dma_start(w_in[:, :, 512 * n:512 * n + 512],
                                     I["w_in"][0][:, 512 * n:512 * n + 512].rearrange(kview, p=P)).then_inc(win_here, 16)
                    for n in range(4):
                        sp.wait_ge(kv_sbuf, n + 1)
                        sp.dma_start(O["k"][P * (n // 2):P * (n // 2) + P, 512 * (n % 2):512 * (n % 2) + 512],
                                     K[:, n // 2, 512 * (n % 2):512 * (n % 2) + 512]).then_inc(kv_out, 16)
                    for n in range(4):
                        sp.wait_ge(kv_sbuf, n + 5)
                        sp.dma_start(O["v"][P * (n // 2):P * (n // 2) + P, 512 * (n % 2):512 * (n % 2) + 512],
                                     V[:, n // 2, 512 * (n % 2):512 * (n % 2) + 512]).then_inc(kv_out, 16)
                    sp.wait_ge(table_set, 4)
                    sp.dma_start(table_d.rearrange("(p q) a -> p (q a)", p=P), tabf[:]).then_inc(table_sent, 16)
                    sp.dma_start(h3_d[TOK:TOK + P // 2, :], zrow[:]).then_inc(table_sent, 16)
                    sp.wait_ge(kt_done, 4)
                    sp.dma_start(w_out, I["w_out"][0].rearrange(kview, p=P)).then_inc(wout_here, 16)
                    sp.dma_start(w_xq, I["w_xq"][0].rearrange(kview, p=P)).then_inc(wxq_here, 16)
                    sp.wait_ge(kv_out, 128)
                    sp.wait_ge(table_sent, 32)

                @block.gpsimd
                def _(pool):
                    pool.memset(ident[:], 0.0).then_inc(ident_set, 1)
                    pool.memset(mhalf[:], -0.5).then_inc(ident_set, 1)
                    pool.memset(ones[:], 1.0).then_inc(ident_set, 1)
                    pool.memset(total[:], 0.0).then_inc(ident_set, 1)
                    pool.memset(zrow[:], 0.0).then_inc(table_set, 1)
                    pool.memset(sgw_s[:], 0.0).then_inc(sgs_zero, 1)
                    pool.iota(tabm[:], [[1, NE * CAP // P]], base=0, channel_multiplier=NE * CAP // P).then_inc(table_set, 1)
                    pool.wait_ge(ident_set, 4)
                    pool.affine_select(out=ident[:], in_=ident[:], compare_op=ALU.not_equal, fill=1.0, base=0,
                                       pattern=[[-1, P]], channel_multiplier=1).then_inc(ident_done, 1)
                    pool.affine_select(out=lower[:], in_=ones[:], compare_op=ALU.is_gt, fill=0.0, base=0,
                                       pattern=[[1, P]], channel_multiplier=-1).then_inc(ident_done, 1)
                    for m in range(2):
                        pool.wait_ge(squares, m + 1)
                        settle(pool)
                        pool.tensor_scalar(rstd[:, m:m + 1], ss[:, m:m + 1], EPS, None, ALU.add).then_inc(eps_added, 1)
                        pool.wait_ge(eps_added, m + 1)
                        pool.tensor_tensor(rstd[:, m:m + 1], rstd[:, m:m + 1], mhalf[:], ALU.pow).then_inc(rstd_done, 1)
                    for n, (w, ready) in enumerate(((sgw, sg_here), (sgw_s, blocks_here))):
                        pool.wait_ge(ready, 16 * (1 if n == 0 else SEQS))
                        pool.affine_select(out=w[:], in_=w[:], compare_op=ALU.is_ge, fill=0.0, base=0,
                                           pattern=[[0, HEADS], [-1, P]], channel_multiplier=1).then_inc(sg_masked, 1)

                @block.scalar
                def _(act):
                    act.dma_start(grow[0:8, :], I["g_mix"][0].rearrange("(k p) -> k p", p=P)).then_inc(small_here, 16)
                    act.dma_start(grow[8:16, :], I["g_xattn"][0].rearrange("(k p) -> k p", p=P)).then_inc(small_here, 16)
                    act.dma_start(grow[16:24, :], I["g_mem"][0].rearrange("(k p) -> k p", p=P)).then_inc(small_here, 16)
                    act.dma_start(prow[0:31, :], I["conv_w"][0]).then_inc(small_here, 16)
                    act.dma_start(prow[31:32, :], I["conv_b"]).then_inc(small_here, 16)
                    act.dma_start(prow[32:33, :], I["ln_conv_g"]).then_inc(small_here, 16)
                    act.dma_start(prow[33:34, :], I["ln_conv_b"]).then_inc(small_here, 16)
                    act.dma_start(hrow[:], I["state_conv"][0].rearrange("(a b) r c -> (b r) a c", a=2)).then_inc(small_here, 16)
                    act.dma_start(sgw[:], I["w_sg"][0].rearrange("h i j -> i h j")).then_inc(sg_here, 16)
                    act.wait_ge(sgs_zero, 1)
                    for s in range(SEQS):
                        r = slice(SLEN * s, SLEN * s + SLEN)
                        act.dma_start(sgw_s[r, :, r], I["w_sg"][0][:, 0:SLEN, 0:SLEN].rearrange("h i j -> i h j")).then_inc(blocks_here, 16)
                    act.dma_start(bsg[:], I["b_sg"][0].rearrange("h i -> i h"), allow_slow_non_contiguous=True).then_inc(small_here, 16)
                    for s in range(SEQS):
                        act.dma_start(bsg_s[SLEN * s:SLEN * s + SLEN, :], I["b_sg"][0][:, 0:SLEN].rearrange("h i -> i h"),
                                      allow_slow_non_contiguous=True).then_inc(small_here, 16)
                    act.dma_start(O["state_s"][:, 0:HIST - SLEN, :], I["state_conv"][0][:, SLEN:HIST, :]).then_inc(hist_out, 16)
                    act.wait_ge(mem_here, 16)
                    for m in range(2):
                        if m:
                            act.wait_ge(turned, 8)
                        act.activation(junk[:], mem[:, m, :], ACT.Square, scale=1 / 32, accum_out=ss[:, m:m + 1]).then_inc(squares, 1)
                        act.wait_ge(rstd_done, m + 1)
                        act.wait_ge(squares, m + 1)
                        act.activation(memn[:], mem[:, m, :], ACT.Copy, scale=rstd[:, m:m + 1]).then_inc(normed, 1)
                        act.wait_ge(const_done, 1)
                        act.wait_ge(turned, 8 * (m + 1))
                        for k in range(KD):
                            act.activation(memT[:, k, P * m:P * m + P], pst[0][:, k, :], ACT.Copy,
                                           scale=gcol[:, 16 + k:17 + k]).then_inc(memT_done, 1)
                    act.wait_ge(hist_out, 16)
                    act.wait_ge(small_here, 16 * 17)

                @block.vector
                def _(dve):
                    dve.wait_ge(table_set, 2)
                    dve.tensor_scalar(tabm[:], tabm[:], P - 1, None, ALU.bitwise_and).then_inc(table_set, 1)
                    dve.wait_ge(table_set, 3)
                    dve.tensor_scalar(tabf[:], tabm[:], float(PAIRS), None, ALU.add).then_inc(table_set, 1)
                    dve.wait_ge(const_psum, 1)
                    dve.tensor_copy(gcol[:], psc[0][:, 0, 0:3 * KD]).then_inc(const_done, 1)
                    dve.wait_ge(const_psum, 2)
                    dve.tensor_copy(pcol[:], psc[1][:, :, 0:34]).then_inc(const_done, 1)
                    for a in range(2):
                        dve.wait_ge(const_psum, 3 + a)
                        dve.tensor_copy(sext[:, :, 4 * a:4 * a + 4, 0:HIST],
                                        psc[a][:, :, 0:120].rearrange("p c (s r) -> p c s r", r=HIST)).then_inc(const_done, 1)
                    dve.wait_ge(const_psum, 5)
                    dve.tensor_copy(sgT[:], psc[0][:]).then_inc(const_done, 1)
                    dve.wait_ge(const_psum, 6)
                    dve.tensor_copy(sgT_s[:], psc[1][:]).then_inc(const_done, 1)
                    for n in range(8):
                        dst = (K if n < 4 else V)[:, n % 4 // 2, 512 * (n % 2):512 * (n % 2) + 512]
                        dve.wait_ge(kv_psum, n + 1)
                        dve.tensor_copy(dst, psk[n % 4][:]).then_inc(kv_sbuf, 1)
                    for n in range(4):
                        dve.wait_ge(kt_psum, n + 1)
                        dve.tensor_copy(KT[:, 4 * (n // 2):4 * (n // 2) + 4, P * (n % 2):P * (n % 2) + P], psk[n][:].rearrange("p (k m) -> p k m", k=4)).then_inc(kt_done, 1)

                @block.tensor
                def _(pe):
                    pe.wait_ge(ident_done, 2)
                    pe.wait_ge(small_here, 16 * 17)
                    pe.transpose(psc[0][:, 0, 0:3 * KD], grow[:], ident[0:3 * KD, 0:3 * KD]).then_inc(const_psum, 1)
                    for c in range(CG):
                        last = pe.transpose(psc[1][:, c, 0:34], prow[:, P * c:P * c + P], ident[0:34, 0:34])
                    last.then_inc(const_psum, 1)
                    for m in range(2):
                        pe.wait_ge(normed, m + 1)
                        if m:
                            pe.wait_ge(memT_done, KD)
                        for k in range(KD):
                            pe.transpose(pst[0][:, k, :], memn[:, P * k:P * k + P], ident[:]).then_inc(turned, 1)
                    for a in range(2):
                        pe.wait_ge(const_done, 1 + a)
                        for c in range(CG):
                            last = pe.transpose(psc[a][:, c, 0:120], hrow[:, a, P * c:P * c + P], ident[0:120, 0:120])
                        last.then_inc(const_psum, 1)
                    for a, w in enumerate((sgw, sgw_s)):
                        pe.wait_ge(const_done, 3 + a)
                        pe.wait_ge(sg_masked, a + 1)
                        for h in range(HEADS):
                            last = pe.transpose(psc[a][:, h, :], w[:, h, :], ident[:])
                        last.then_inc(const_psum, 1)
                    pe.wait_ge(memT_done, 2 * KD)
                    for n in range(8):
                        w = w_mk if n < 4 else w_mv
                        if n % 4 == 0:
                            pe.wait_ge(wmk_here if n < 4 else wmv_here, 16)
                        if n >= 4:
                            pe.wait_ge(kv_sbuf, n - 3)
                        m, c = n % 4 // 2, 512 * (n % 2)
                        for k in range(KD):
                            last = pe.matmul(psk[n % 4][:], memT[:, k, P * m:P * m + P], w[:, k, c:c + 512],
                                             start=(k == 0), stop=(k == KD - 1))
                        last.then_inc(kv_psum, 1)
                    for n in range(4):
                        pe.wait_ge(kv_sbuf, n + 5)
                        for j in range(4):
                            k = 4 * (n // 2) + j
                            last = pe.transpose(psk[n][:, P * j:P * j + P], K[:, n % 2, P * k:P * k + P], ident[:])
                        last.then_inc(kt_psum, 1)

        with one_stage() as st:
            sb, pb, sem = alloc(st)
            x_in = [sb(f"a_x{i}", [P, D]) for i in range(1)]
            xn = x_in[0]
            hT = [sb(f"a_hT{i}", [P, KD, P]) for i in range(1)]
            hT = [hT[0], sb("a_hT1", [P, KD, P])]
            junk = sb("a_junk", [P, D])
            sig = sb("a_sig", [P, DC])
            a_tok = [sb(f"a_tok{i}", [P, DC]) for i in range(2)]
            stage = [sb(f"a_stage{i}", [P, CG, P]) for i in range(2)]
            aext = sb("aext", [P, CG, HIST + 2 * P])
            yacc = sb("yacc", [P, 2, 2 * P])
            ybuf = sb("ybuf", [P, CG, 2 * P])
            u_sb = sb("a_u", [P, DC])
            vn = sb("a_vn", [P, DC])
            b_tok = sb("a_btok", [P, DC])
            maT = sb("a_maT", [P, CG, P])
            mbT = sb("a_mbT", [P, CG, P])
            gv = sb("gv", [P, DC])
            bv = sb("bv", [P, DC])
            ss = sb("a_ss", [P, 2])
            rs = sb("a_rs", [P, 2])
            vst = sb("a_vst", [P, 6])
            vmv = sb("a_vmv", [P, 2])
            vrs = sb("a_vrs", [P, 2])
            yst = sb("a_yst", [P, 6])
            ymv = sb("a_ymv", [P, 2])
            yrs = sb("a_yrs", [P, 2])
            yn = junk[:, 0:DC]
            psz = [pb(f"a_psz{i}", [P, 512]) for i in range(4)]
            pst = pb("a_pst", [P, 4, P])
            psx = pb("a_psx", [P, CG, P])
            psg = pb("a_psg", [P, HEADS, P])
            psy = pb("a_psy", [P, CG, P])
            names = ("x_here0 v_consts squares eps rstd normed turned hT_done gate_psum val_psum v_psum u_psum tanh_done "
                     "sig_done a_done aT_psum stage_full ext_ready conv_step y_ready vstat vagg veps vrstd vnmr vnormed "
                     "vgain v_done sg_psum u_done b_done bT_psum mb_done mb_out yT_psum ystat yagg yeps yrstd ynmr "
                     "ynormed ynT_psum ma_done ma_out state_out halo").split()
            S = {n: sem("a_" + n) for n in names}
            GATE, VAL, VV, UU = range(4)
            COL = [512, 0, 1536, 1024]

            with nc.Block() as block:
                @block.sync
                def _(sp):
                    sp.dma_start(gv[:], I["ln_v_g"].partition_broadcast(P).rearrange("p a d -> p (a d)")).then_inc(S["v_consts"], 16)
                    sp.dma_start(bv[:], I["ln_v_b"].partition_broadcast(P).rearrange("p a d -> p (a d)")).then_inc(S["v_consts"], 16)

                    def load(t):
                        need(sp, S["turned"], 2 * t.v)
                        load_x(sp, x_in[0][:], t).then_inc(S["x_here0"], 16)

                    def store_b(t):
                        sp.wait_ge(S["mb_done"], t.v + 1)
                        sp.dma_start(row(mixb_d, t), mbT[:].rearrange("p c n -> p (c n)")).then_inc(S["mb_out"], 16)

                    def store_a(t):
                        sp.wait_ge(S["ma_done"], t.v + 1)
                        sp.dma_start(row(mixa_d, t), maT[:].rearrange("p c n -> p (c n)")).then_inc(S["ma_out"], 16)

                    def step(s):
                        if s.exists() and isinstance(s.v, int) and s.v == 0:
                            load(s)
                        if s.at(1).exists():
                            load(s.at(1))
                        if s.at(-1).exists():
                            store_b(s.at(-1))
                        if isinstance(s.v, int) and s.v == PT - 1:
                            sp.wait_ge(S["a_done"], PT)
                            sp.dma_start(O["state_p"], a_tok[1][P - HIST:P, :]).then_inc(S["state_out"], 16)
                        if isinstance(s.v, int) and s.v == PT:
                            sp.wait_ge(S["a_done"], NT)
                            for q in range(SEQS):
                                sp.dma_start(O["state_s"][q, HIST - SLEN:HIST, :], a_tok[0][SLEN * q:SLEN * q + SLEN, :]).then_inc(S["state_out"], 16)
                            sp.wait_ge(S["v_done"], NT)
                            sp.dma_start(O["sgv"], vn[:]).then_inc(S["state_out"], 16)
                        if s.at(-4).exists():
                            store_a(s.at(-4))
                    steps(sp, step, 4, 5, 21)
                    sp.wait_ge(S["state_out"], 16 * 10)
                    sp.wait_ge(S["ma_out"], 16 * NT)
                    sp.wait_ge(S["mb_out"], 16 * NT)

                @block.gpsimd
                def _(pool):
                    def rms(t):
                        pool.wait_ge(S["squares"], t.v + 1)
                        settle(pool)
                        pool.tensor_scalar(rs[:, t.par:t.par + 1], ss[:, t.par:t.par + 1], EPS, None, ALU.add).then_inc(S["eps"], 1)
                        pool.wait_ge(S["eps"], t.v + 1)
                        pool.tensor_tensor(rs[:, t.par:t.par + 1], rs[:, t.par:t.par + 1], mhalf[:], ALU.pow).then_inc(S["rstd"], 1)

                    def norm_consts(t, mv, r, stat, used, eps, rstd, nmr):
                        need(pool, S[used], t.v)
                        pool.wait_ge(S[stat], t.v + 1)
                        settle(pool)
                        pool.tensor_scalar(r[:, 0:1], mv[:, 1:2], EPS, None, ALU.add).then_inc(S[eps], 1)
                        pool.wait_ge(S[eps], t.v + 1)
                        pool.tensor_tensor(r[:, 0:1], r[:, 0:1], mhalf[:], ALU.pow).then_inc(S[rstd], 1)
                        pool.wait_ge(S[rstd], t.v + 1)
                        settle(pool)
                        pool.tensor_scalar(r[:, 1:2], mv[:, 0:1], r[:, 0:1], -1.0, ALU.mult, ALU.mult).then_inc(S[nmr], 1)

                    def step(s):
                        if isinstance(s.v, int) and s.v == 0:
                            rms(s)
                            pool.wait_ge(S["v_consts"], 32)
                        if s.exists():
                            pool.wait_ge(S["tanh_done"], s.v + 1)
                            settle(pool)
                            pool.tensor_scalar(sig[:], sig[:], 0.5, 0.5, ALU.mult, ALU.add).then_inc(S["sig_done"], 1)
                        if s.at(1).exists():
                            rms(s.at(1))
                        if s.at(-4).exists():
                            norm_consts(s.at(-4), ymv, yrs, "yagg", "ynormed", "yeps", "yrstd", "ynmr")
                        if s.exists():
                            norm_consts(s, vmv, vrs, "vagg", "vnormed", "veps", "vrstd", "vnmr")
                            pool.wait_ge(S["vnormed"], s.v + 1)
                            pool.tensor_tensor(vn[:], vn[:], gv[:], ALU.mult).then_inc(S["vgain"], 1)
                            pool.wait_ge(S["vgain"], s.v + 1)
                            pool.tensor_tensor(vn[:], vn[:], bv[:], ALU.add).then_inc(S["v_done"], 1)
                    steps(pool, step, 4, 6, 21)

                @block.scalar
                def _(act):
                    def square(t):
                        act.wait_ge(S["x_here0"], 16 * (t.v + 1))
                        need(act, S["normed"], t.v)
                        act.activation(junk[:], x_in[0][:], ACT.Square, scale=1 / 32, accum_out=ss[:, t.par:t.par + 1]).then_inc(S["squares"], 1)

                    def norm(t):
                        act.wait_ge(S["rstd"], t.v + 1)
                        act.wait_ge(S["squares"], t.v + 1)
                        act.activation(xn[:], x_in[0][:], ACT.Copy, scale=rs[:, t.par:t.par + 1]).then_inc(S["normed"], 1)

                    def evac_hT(t, half):
                        act.wait_ge(S["turned"], 2 * t.v + half + 1)
                        if half == 0:
                            need(act, S["u_psum"], t.v - 1)
                        for j in range(4):
                            k = 4 * half + j
                            last = act.activation(hT[t.par][:, k, :], pst[:, j, :], ACT.Copy, scale=gcol[:, k:k + 1])
                        last.then_inc(S["hT_done"], 1)

                    def step(s):
                        if isinstance(s.v, int) and s.v == 0:
                            square(s)
                            norm(s)
                            evac_hT(s, 0)
                            evac_hT(s, 1)
                        if s.exists():
                            act.wait_ge(S["gate_psum"], s.v + 1)
                            need(act, S["a_done"], s.v)
                            act.activation(sig[:], psz[GATE][:], ACT.Tanh, scale=0.5).then_inc(S["tanh_done"], 1)
                        t = s.at(1)
                        if t.exists():
                            need(act, S["ynT_psum"], t.v - 5)
                            square(t)
                            norm(t)
                        t = s.at(-1)
                        if t.exists():
                            act.wait_ge(S["bT_psum"], t.v + 1)
                            need(act, S["mb_out"], 16 * t.v)
                            act.activation(mbT[:], psx[:], ACT.Copy).then_inc(S["mb_done"], 1)
                        t = s.at(-4)
                        if t.exists():
                            act.wait_ge(S["ynmr"], t.v + 1)
                            act.wait_ge(S["squares"], min_tile(s.v + 2))
                            act.activation(yn, psy[:].rearrange("p c n -> p (c n)"), ACT.Identity, bias=yrs[:, 1:2],
                                           scale=yrs[:, 0:1]).then_inc(S["ynormed"], 1)
                        if s.at(1).exists():
                            evac_hT(s.at(1), 0)
                        if s.exists():
                            act.wait_ge(S["vnmr"], s.v + 1)
                            need(act, S["sg_psum"], s.v)
                            act.activation(vn[:], psz[VV][:], ACT.Identity, bias=vrs[:, 1:2], scale=vrs[:, 0:1]).then_inc(S["vnormed"], 1)
                        if s.at(1).exists():
                            evac_hT(s.at(1), 1)
                        t = s.at(-4)
                        if t.exists():
                            act.wait_ge(S["ynT_psum"], t.v + 1)
                            need(act, S["ma_out"], 16 * t.v)
                            for c in range(CG):
                                last = act.activation(maT[:, c, :], psx[:, c, :], ACT.Silu, bias=pcol[:, c, 33:34], scale=pcol[:, c, 32:33])
                            last.then_inc(S["ma_done"], 1)
                        if s.exists():
                            act.wait_ge(S["u_psum"], s.v + 1)
                            need(act, S["b_done"], s.v)
                            act.activation(u_sb[:], psz[UU][:], ACT.Copy).then_inc(S["u_done"], 1)
                            act.wait_ge(S["aT_psum"], s.v + 1)
                            if isinstance(s.v, int) and s.v == PT:
                                act.activation(sext[:, :, :, HIST:HIST + SLEN],
                                               psx[:].rearrange("p c (s r) -> p c s r", r=SLEN), ACT.Copy).then_inc(S["stage_full"], 1)
                            else:
                                need(act, S["ext_ready"], 2 * s.half)
                                act.activation(stage[s.par][:], psx[:], ACT.Copy).then_inc(S["stage_full"], 1)

                    def min_tile(v):
                        return v if not isinstance(v, int) else min(v, NT)
                    steps(act, step, 4, 6, 21)

                @block.vector
                def _(dve):
                    def conv(pair_half, first, taps):
                        base = pair_half * (4 * TAPS) + first * TAPS
                        for k in taps:
                            for i in range(2):
                                c = first + i
                                w = pcol[:, c, k:k + 1]
                                src = aext[:, c, k:k + 2 * P]
                                if k == 0:
                                    need(dve, S["conv_step"], base + i - 1)
                                    ins = dve.tensor_scalar(yacc[:, i, :], src, w, pcol[:, c, 31:32], ALU.mult, ALU.add)
                                else:
                                    dve.wait_ge(S["conv_step"], base + 2 * k - 1 + i)
                                    out = yacc[:, i, :]
                                    if k == TAPS - 1:
                                        if i == 0:
                                            need(dve, S["yT_psum"], 2 * pair_half)
                                        out = ybuf[:, c, :]
                                    ins = dve.scalar_tensor_tensor(out=out, in0=src, scalar=w, in1=yacc[:, i, :], op0=ALU.mult, op1=ALU.add)
                                ins.then_inc(S["conv_step"], 1)

                    def conv_sample():
                        base = (PT // 2) * 4 * TAPS
                        for k in range(TAPS):
                            for c in range(CG):
                                w = pcol[:, c, k:k + 1]
                                src = sext[:, c, :, k:k + SLEN]
                                acc = yacc[:, c // 2, P * (c % 2):P * (c % 2) + P].rearrange("p (s r) -> p s r", r=SLEN)
                                if k == 0:
                                    ins = dve.tensor_scalar(acc, src, w, pcol[:, c, 31:32], ALU.mult, ALU.add)
                                else:
                                    dve.wait_ge(S["conv_step"], base + 4 * (k - 1) + c + 1)
                                    out = acc
                                    if k == TAPS - 1:
                                        if c == 0:
                                            dve.wait_ge(S["yT_psum"], PT)
                                        out = ybuf[:, c, 0:P].rearrange("p (s r) -> p s r", r=SLEN)
                                    ins = dve.scalar_tensor_tensor(out=out, in0=src, scalar=w, in1=acc, op0=ALU.mult, op1=ALU.add)
                                ins.then_inc(S["conv_step"], 1)

                    dve.memset(aext[:, :, 0:HIST], 0.0).then_inc(S["halo"], 1)

                    def step(s):
                        static = isinstance(s.v, int)
                        if s.exists():
                            dve.wait_ge(S["val_psum"], s.v + 1)
                            dve.wait_ge(S["sig_done"], s.v + 1)
                            need(dve, S["aT_psum"], s.v - 1)
                            dve.tensor_tensor(a_tok[s.par][:], psz[VAL][:], sig[:], ALU.mult).then_inc(S["a_done"], 1)
                        t = s.at(-1)
                        if t.exists():
                            bias = bsg_s if isinstance(t.v, int) and t.v == PT else bsg
                            dve.wait_ge(S["sg_psum"], t.v + 1)
                            dve.wait_ge(S["u_done"], t.v + 1)
                            need(dve, S["bT_psum"], t.v)
                            for h in range(HEADS):
                                c = slice(P * h, P * h + P)
                                last = dve.scalar_tensor_tensor(out=b_tok[:, c], in0=psg[:, h, :], scalar=bias[:, h:h + 1],
                                                                in1=u_sb[:, c], op0=ALU.add, op1=ALU.mult)
                            last.then_inc(S["b_done"], 1)
                        t = s.at(-4)
                        if t.exists():
                            dve.wait_ge(S["yT_psum"], t.v + 1)
                            dve.bn_stats(yst[:], psy[:].rearrange("p c n -> p (c n)")).then_inc(S["ystat"], 1)
                            dve.wait_ge(S["ystat"], t.v + 1)
                            need(dve, S["ynmr"], t.v)
                            settle(dve)
                            dve.bn_aggr(ymv[:], yst[:]).then_inc(S["yagg"], 1)
                        q = s.at(-2)
                        if q.exists(PT) and s.par == 0:
                            if static and s.v == 2:
                                dve.wait_ge(S["halo"], 1)
                            else:
                                dve.wait_ge(S["conv_step"], q.half * 4 * TAPS)
                                dve.tensor_copy(aext[:, :, 0:HIST], aext[:, :, 2 * P:2 * P + HIST]).then_inc(S["halo"], 1)
                                dve.wait_ge(S["halo"], q.half + 1)
                            for i in range(2):
                                dve.wait_ge(S["stage_full"], q.v + i + 1)
                                dve.tensor_copy(aext[:, :, HIST + P * i:HIST + P * i + P], stage[i][:]).then_inc(S["ext_ready"], 1)
                            dve.wait_ge(S["ext_ready"], q.v + 2)
                        q = s.at(-2 - s.par)
                        if q.exists(PT):
                            conv(q.half, 2 * s.par, range(0, 16))
                        if static and s.v == PT + 2:
                            dve.wait_ge(S["stage_full"], NT)
                            dve.wait_ge(S["conv_step"], PT // 2 * 4 * TAPS)
                            conv_sample()
                        if s.exists():
                            dve.wait_ge(S["v_psum"], s.v + 1)
                            dve.bn_stats(vst[:], psz[VV][:]).then_inc(S["vstat"], 1)
                            dve.wait_ge(S["vstat"], s.v + 1)
                            need(dve, S["vnmr"], s.v)
                            settle(dve)
                            dve.bn_aggr(vmv[:], vst[:]).then_inc(S["vagg"], 1)
                        if q.exists(PT):
                            conv(q.half, 2 * s.par, range(16, TAPS))
                    steps(dve, step, 4, 6, 21)

                @block.tensor
                def _(pe):
                    def turn_x(t, half):
                        pe.wait_ge(S["normed"], t.v + 1)
                        need(pe, S["hT_done"], 2 * t.v + half)
                        for j in range(4):
                            k = 4 * half + j
                            last = pe.transpose(pst[:, j, :], xn[:, P * k:P * k + P], ident[:])
                        last.then_inc(S["turned"], 1)

                    def project(t, bank, done, free):
                        if isinstance(t.v, int) and t.v == 0:
                            pe.wait_ge(win_here, 64)
                        if bank == GATE:
                            pe.wait_ge(S["hT_done"], 2 * t.v + 2)
                        need(pe, S[free], t.v)
                        for k in range(KD):
                            last = pe.matmul(psz[bank][:], hT[t.par][:, k, :], w_in[:, k, COL[bank]:COL[bank] + 512],
                                             start=(k == 0), stop=(k == KD - 1))
                        last.then_inc(S[done], 1)

                    def turn_y(t):
                        if isinstance(t.v, int) and t.v == PT:
                            pe.wait_ge(S["conv_step"], PT // 2 * 4 * TAPS + CG * TAPS)
                        else:
                            pe.wait_ge(S["conv_step"], (t.half + 1) * 4 * TAPS)
                        need(pe, S["ynormed"], t.v)
                        for c in range(CG):
                            last = pe.transpose(psy[:, c, :], ybuf[:, c, P * t.par:P * t.par + P], ident[:])
                        last.then_inc(S["yT_psum"], 1)

                    def step(s):
                        if isinstance(s.v, int) and s.v == 0:
                            turn_x(s, 0)
                            turn_x(s, 1)
                        if s.exists():
                            project(s, GATE, "gate_psum", "tanh_done")
                        t = s.at(-4)
                        if t.exists():
                            turn_y(t)
                        t = s.at(-1)
                        if t.exists():
                            w = sgT_s if isinstance(t.v, int) and t.v == PT else sgT
                            pe.wait_ge(S["v_done"], t.v + 1)
                            need(pe, S["b_done"], t.v)
                            for h in range(HEADS):
                                last = pe.matmul(psg[:, h, :], w[:, h, :], vn[:, P * h:P * h + P], start=True, stop=True)
                            last.then_inc(S["sg_psum"], 1)
                        if s.exists():
                            project(s, VAL, "val_psum", "a_done")
                        if t.exists():
                            pe.wait_ge(S["b_done"], t.v + 1)
                            pe.wait_ge(S["stage_full"], t.v + 1)
                            for c in range(CG):
                                last = pe.transpose(psx[:, c, :], b_tok[:, P * c:P * c + P], ident[:])
                            last.then_inc(S["bT_psum"], 1)
                        if s.at(1).exists():
                            turn_x(s.at(1), 0)
                        if s.exists():
                            project(s, VV, "v_psum", "vnormed")
                        if s.at(1).exists():
                            turn_x(s.at(1), 1)
                        t = s.at(-4)
                        if t.exists():
                            pe.wait_ge(S["ynormed"], t.v + 1)
                            if s.at(-1).exists():
                                pe.wait_ge(S["mb_done"], s.v)
                            else:
                                pe.wait_ge(S["mb_done"], NT)
                                need(pe, S["ma_done"], t.v)
                            for c in range(CG):
                                last = pe.transpose(psx[:, c, :], yn[:, P * c:P * c + P], ident[:])
                            last.then_inc(S["ynT_psum"], 1)
                        if s.exists():
                            project(s, UU, "u_psum", "u_done")
                            pe.wait_ge(S["a_done"], s.v + 1)
                            need(pe, S["ma_done"], s.v - 3)
                            need(pe, S["mb_done"], s.v)
                            for c in range(CG):
                                last = pe.transpose(psx[:, c, :], a_tok[s.par][:, P * c:P * c + P], ident[:])
                            last.then_inc(S["aT_psum"], 1)
                    steps(pe, step, 4, 6, 21)
        mix_stack.close()

        q_stack = ExitStack()
        sbq, _, _ = alloc(q_stack)
        qT = sbq("qT", [P, 8, P])
        with one_stage() as st:
            sb, pb, sem = alloc(st)
            mixT = [sb(f"b_mixT{i}", [P, 2, CG, P]) for i in range(2)]
            x_in = sb("b_x", [P, D])
            x1 = [sb(f"b_x1{i}", [P, D]) for i in range(2)]
            xn = sb("b_xn", [P, D])
            h2T = sb("b_h2T", [P, KD, P])
            prob = sb("b_prob", [P, HEADS, NMEM])
            pT = sb("b_pT", [P, 8, P])
            oT = sb("b_oT", [P, 8, P])
            ss = sb("b_ss", [P, 1])
            rs = sb("b_rs", [P, 2])
            mx = sb("b_mx", [P, HEADS])
            nb = sb("b_nb", [P, HEADS])
            sm = sb("b_sm", [P, HEADS])
            rc = sb("b_rc", [P, HEADS])
            pso = pb("b_pso", [P, D])
            pss = pb("b_pss", [P, HEADS, NMEM])
            psq = pb("b_psq", [P, 8, P])
            pst = pb("b_pst", [P, 8, P])
            names = ("x_here wo_psum x1_done squares eps rstd normed turned h2T_done q_psum qT_done "
                     "s_psum max_done nb_done exp_done rc_done prob_done pT_psum pT_done o_psum oT_done oT_out").split()
            S = {n: sem("b_" + n) for n in names}
            mix_here = [sem(f"b_mix_here{i}") for i in range(2)]
            x1_out = [sem(f"b_x1_out{i}") for i in range(2)]
            with nc.Block() as block:
                @block.sync
                def _(sp):
                    sp.dma_start(w_xo, I["w_xo"][0].rearrange(kview, p=P)).then_inc(wxo_here, 16)

                    def load(t):
                        need(sp, S["wo_psum"], t.v - 1)
                        sp.dma_start(mixT[t.par][:, 0, :, :].rearrange("p c n -> p (c n)"), row(mixa_d, t)).then_inc(mix_here[t.par], 16)
                        sp.dma_start(mixT[t.par][:, 1, :, :].rearrange("p c n -> p (c n)"), row(mixb_d, t)).then_inc(mix_here[t.par], 16)
                        need(sp, S["x1_done"], t.v)
                        load_x(sp, x_in[:], t).then_inc(S["x_here"], 16)

                    def step(s):
                        if isinstance(s.v, int) and s.v == 0:
                            load(s)
                        if s.at(1).exists():
                            load(s.at(1))
                        if s.exists():
                            sp.wait_ge(S["x1_done"], s.v + 1)
                            sp.dma_start(row(x1_d, s), x1[s.par][:]).then_inc(x1_out[s.par], 16)
                        t = s.at(-2)
                        if t.exists(PT):
                            sp.wait_ge(S["oT_done"], t.v + 1)
                            sp.dma_start(row(oT_d, t), oT[:].rearrange("p c n -> p (c n)")).then_inc(S["oT_out"], 16)
                    steps(sp, step, 2, 6, NT + 1)
                    sp.wait_ge(x1_out[0], 16 * 9)
                    sp.wait_ge(x1_out[1], 16 * 8)
                    sp.wait_ge(S["oT_out"], 16 * PT)

                @block.gpsimd
                def _(pool):
                    def step(t):
                        pool.wait_ge(S["squares"], t.v + 1)
                        need(pool, S["normed"], t.v)
                        settle(pool)
                        pool.tensor_scalar(rs[:, 0:1], ss[:], EPS, None, ALU.add).then_inc(S["eps"], 1)
                        pool.wait_ge(S["eps"], t.v + 1)
                        pool.tensor_tensor(rs[:, 1:2], rs[:, 0:1], mhalf[:], ALU.pow).then_inc(S["rstd"], 1)
                    steps(pool, step, 2, 7, NT)

                @block.scalar
                def _(act):
                    def step(s):
                        if s.exists():
                            act.wait_ge(S["x1_done"], s.v + 1)
                            need(act, S["turned"], s.v)
                            act.activation(xn[:], x1[s.par][:], ACT.Square, scale=1 / 32, accum_out=ss[:]).then_inc(S["squares"], 1)
                            act.wait_ge(S["rstd"], s.v + 1)
                            act.wait_ge(S["squares"], s.v + 1)
                            act.activation(xn[:], x1[s.par][:], ACT.Copy, scale=rs[:, 1:2]).then_inc(S["normed"], 1)
                        t = s.at(-2)
                        if t.exists(PT):
                            act.wait_ge(S["pT_psum"], t.v + 1)
                            need(act, S["o_psum"], t.v)
                            act.activation(pT[:], psq[:], ACT.Copy).then_inc(S["pT_done"], 1)
                        t = s.at(-1)
                        if t.exists(PT):
                            act.wait_ge(S["nb_done"], t.v + 1)
                            need(act, S["pT_psum"], t.v)
                            need(act, S["prob_done"], t.v)
                            for h in range(HEADS):
                                last = act.activation(prob[:, h, :], pss[:, h, :], ACT.Exp, bias=nb[:, h:h + 1], scale=SCALE,
                                                      accum_out=sm[:, h:h + 1])
                            last.then_inc(S["exp_done"], 1)
                        t = s.at(-2)
                        if t.exists(PT):
                            act.wait_ge(S["o_psum"], t.v + 1)
                            need(act, S["oT_out"], 16 * t.v)
                            act.activation(oT[:], pso[:].rearrange("p (c n) -> p c n", c=8), ACT.Copy).then_inc(S["oT_done"], 1)
                        if s.exists():
                            act.wait_ge(S["q_psum"], s.v + 1)
                            need(act, S["s_psum"], s.v)
                            act.activation(qT[:], psq[:], ACT.Copy).then_inc(S["qT_done"], 1)
                    steps(act, step, 2, 7, NT + 1)

                @block.vector
                def _(dve):
                    def step(s):
                        if s.exists():
                            dve.wait_ge(S["wo_psum"], s.v + 1)
                            dve.wait_ge(S["x_here"], 16 * (s.v + 1))
                            need(dve, S["normed"], s.v - 1)
                            need(dve, x1_out[s.par], 16 * s.half)
                            dve.tensor_tensor(x1[s.par][:], pso[:], x_in[:], ALU.add).then_inc(S["x1_done"], 1)
                        t = s.at(-1)
                        if t.exists(PT):
                            dve.wait_ge(S["s_psum"], t.v + 1)
                            need(dve, S["nb_done"], t.v)
                            dve.tensor_reduce(mx[:], pss[:], X, ALU.max).then_inc(S["max_done"], 1)
                            dve.wait_ge(S["max_done"], t.v + 1)
                            need(dve, S["exp_done"], t.v)
                            dve.tensor_scalar(nb[:], mx[:], -SCALE, None, ALU.mult).then_inc(S["nb_done"], 1)
                        if s.exists():
                            dve.wait_ge(S["turned"], s.v + 1)
                            need(dve, S["q_psum"], s.v)
                            dve.tensor_tensor(h2T[:], pst[:], gcol[:, 8:16].unsqueeze(2).to_broadcast([P, KD, P]), ALU.mult).then_inc(S["h2T_done"], 1)
                        if t.exists(PT):
                            dve.wait_ge(S["exp_done"], t.v + 1)
                            need(dve, S["prob_done"], t.v)
                            dve.reciprocal(rc[:], sm[:]).then_inc(S["rc_done"], 1)
                            dve.wait_ge(S["rc_done"], t.v + 1)
                            dve.tensor_tensor(prob[:], prob[:], rc[:].unsqueeze(2).to_broadcast([P, HEADS, NMEM]), ALU.mult).then_inc(S["prob_done"], 1)
                    steps(dve, step, 2, 7, NT + 1)

                @block.tensor
                def _(pe):
                    pe.wait_ge(wout_here, 16)
                    pe.wait_ge(wxq_here, 16)

                    def step(s):
                        if s.exists():
                            pe.wait_ge(mix_here[s.par], 32 * (s.half + 1))
                            need(pe, S["x1_done"], s.v)
                            need(pe, S["oT_done"], s.v - 2)
                            for n in range(2):
                                for k in range(KD):
                                    last = pe.matmul(pso[:, 512 * n:512 * n + 512], mixT[s.par][:, k // 4, k % 4, :],
                                                     w_out[:, k, 512 * n:512 * n + 512], start=(k == 0), stop=(k == KD - 1))
                            last.then_inc(S["wo_psum"], 1)
                        t = s.at(-1)
                        if t.exists(PT):
                            pe.wait_ge(S["qT_done"], t.v + 1)
                            need(pe, S["exp_done"], t.v)
                            for h in range(HEADS):
                                for k in range(2):
                                    last = pe.matmul(pss[:, h, :], qT[:, 2 * h + k, :], KT[:, 2 * h + k, :], start=(k == 0), stop=(k == 1))
                            last.then_inc(S["s_psum"], 1)
                        t = s.at(-2)
                        if t.exists(PT):
                            pe.wait_ge(S["prob_done"], t.v + 1)
                            pe.wait_ge(S["qT_done"], t.v + 2)
                            for h in range(HEADS):
                                for m in range(2):
                                    last = pe.transpose(psq[:, 2 * h + m, :], prob[:, h, P * m:P * m + P], ident[:])
                            last.then_inc(S["pT_psum"], 1)
                        if s.exists():
                            pe.wait_ge(S["normed"], s.v + 1)
                            need(pe, S["h2T_done"], s.v)
                            for k in range(KD):
                                last = pe.transpose(pst[:, k, :], xn[:, P * k:P * k + P], ident[:])
                            last.then_inc(S["turned"], 1)
                        if t.exists(PT):
                            pe.wait_ge(S["pT_done"], t.v + 1)
                            if s.exists():
                                pe.wait_ge(S["x1_done"], s.v + 1)
                            need(pe, S["oT_done"], t.v)
                            for c in range(8):
                                for m in range(2):
                                    last = pe.matmul(pso[:, P * c:P * c + P], V[:, m, P * c:P * c + P], pT[:, c // 2 * 2 + m, :],
                                                     start=(m == 0), stop=(m == 1))
                            last.then_inc(S["o_psum"], 1)
                        if s.exists():
                            pe.wait_ge(S["h2T_done"], s.v + 1)
                            need(pe, S["qT_done"], s.v)
                            if t.exists(PT):
                                pe.wait_ge(S["pT_done"], t.v + 1)
                            for c in range(8):
                                for k in range(KD):
                                    last = pe.matmul(psq[:, c, :], w_xq[:, k, P * c:P * c + P], h2T[:, k, :],
                                                     start=(k == 0), stop=(k == KD - 1))
                            last.then_inc(S["q_psum"], 1)
                    steps(pe, step, 2, 7, NT + 1)
        with one_stage() as st:
            sb, pb, sem = alloc(st)
            kv = [sb(f"s_kv{i}", [P, 2, D]) for i in range(2)]
            KTs = sb("s_KT", [P, 8, NMEM])
            sT = sb("s_sT", [P, 8, P])
            prob = sb("s_prob", [P, HEADS, NMEM])
            pT = sb("s_pT", [P, 8, P])
            oT = sb("s_oT", [P, 8, P])
            mx = sb("s_mx", [P, HEADS])
            nb = sb("s_nb", [P, HEADS])
            sm = sb("s_sm", [P, HEADS])
            rc = sb("s_rc", [P, HEADS])
            psa = pb("s_psa", [P, 8, P])
            psb = pb("s_psb", [P, 8, P])
            pss = pb("s_pss", [P, 8, P])
            pso = pb("s_pso", [P, 8, P])
            kv_here = [sem(f"s_kv_here{i}") for i in range(2)]
            S = {n: sem("s_" + n) for n in ("ka_psum kb_psum ka_done kb_done s_psum o_psum sT_done s_back max_done nb_done "
                                            "exp_done rc_done prob_done pT_psum pT_done oT_done oT_out").split()}
            with nc.Block() as block:
                @block.sync
                def _(sp):
                    def load(cache, s, used):
                        need(sp, used, s.v - 1)
                        sp.dma_start(kv[s.par][:], I[cache][0][bass.ds(s.v, 1), :, :, :].rearrange("a (m p) h d -> p (a m) (h d)", p=P)).then_inc(kv_here[s.par], 16)
                    steps(sp, lambda s: load("cache_mem_k", s, S["kb_psum"]), 2, 3, SEQS)
                    sp.wait_ge(S["kb_psum"], SEQS)
                    steps(sp, lambda s: load("cache_mem_v", s, S["o_psum"]), 2, 3, SEQS)
                    sp.wait_ge(S["oT_done"], 1)
                    sp.dma_start(oT_d[PT, :, :], oT[:].rearrange("p c n -> p (c n)")).then_inc(S["oT_out"], 16)
                    sp.wait_ge(S["oT_out"], 16)

                @block.scalar
                def _(act):
                    def step(s):
                        act.wait_ge(S["ka_psum"], s.v + 1)
                        need(act, S["s_psum"], s.v)
                        act.activation(KTs[:, :, 0:P], psa[:], ACT.Copy).then_inc(S["ka_done"], 1)
                    steps(act, step, 2, 3, SEQS)
                    act.wait_ge(S["nb_done"], 1)
                    for h in range(HEADS):
                        last = act.activation(prob[:, h, :], pss[:, 2 * h:2 * h + 2, :].rearrange("p a n -> p (a n)"), ACT.Exp,
                                              bias=nb[:, h:h + 1], scale=SCALE, accum_out=sm[:, h:h + 1])
                    last.then_inc(S["exp_done"], 1)
                    act.wait_ge(S["pT_psum"], 1)
                    act.activation(pT[:], psa[:], ACT.Copy).then_inc(S["pT_done"], 1)
                    act.wait_ge(S["o_psum"], SEQS)
                    act.activation(oT[:], pso[:], ACT.Copy).then_inc(S["oT_done"], 1)

                @block.vector
                def _(dve):
                    def step(s):
                        dve.wait_ge(S["kb_psum"], s.v + 1)
                        need(dve, S["s_psum"], s.v)
                        dve.tensor_copy(KTs[:, :, P:2 * P], psb[:]).then_inc(S["kb_done"], 1)
                    steps(dve, step, 2, 3, SEQS)
                    dve.wait_ge(S["s_psum"], SEQS)
                    dve.tensor_copy(sT[:], pso[:]).then_inc(S["sT_done"], 1)
                    dve.wait_ge(S["s_back"], 1)
                    dve.tensor_reduce(mx[:], pss[:].rearrange("p (h m) n -> p h (m n)", m=2), X, ALU.max).then_inc(S["max_done"], 1)
                    dve.wait_ge(S["max_done"], 1)
                    dve.tensor_scalar(nb[:], mx[:], -SCALE, None, ALU.mult).then_inc(S["nb_done"], 1)
                    dve.wait_ge(S["exp_done"], 1)
                    dve.reciprocal(rc[:], sm[:]).then_inc(S["rc_done"], 1)
                    dve.wait_ge(S["rc_done"], 1)
                    dve.tensor_tensor(prob[:], prob[:], rc[:].unsqueeze(2).to_broadcast([P, HEADS, NMEM]), ALU.mult).then_inc(S["prob_done"], 1)

                @block.tensor
                def _(pe):
                    def step(s):
                        pe.wait_ge(kv_here[s.par], 16 * (s.half + 1))
                        need(pe, S["ka_done"], s.v)
                        for k in range(8):
                            last = pe.transpose(psa[:, k, :], kv[s.par][:, 0, P * k:P * k + P], ident[:])
                        last.then_inc(S["ka_psum"], 1)
                        need(pe, S["kb_done"], s.v)
                        for k in range(8):
                            last = pe.transpose(psb[:, k, :], kv[s.par][:, 1, P * k:P * k + P], ident[:])
                        last.then_inc(S["kb_psum"], 1)
                        pe.wait_ge(S["ka_done"], s.v + 1)
                        pe.wait_ge(S["kb_done"], s.v + 1)
                        cols = bass.ds(SLEN * s.v, SLEN)
                        for h in range(HEADS):
                            for m in range(2):
                                for k in range(2):
                                    last = pe.matmul(pso[:, 2 * h + m, cols], KTs[:, 2 * h + k, P * m:P * m + P], qT[:, 2 * h + k, cols],
                                                     start=(k == 0), stop=(k == 1))
                        last.then_inc(S["s_psum"], 1)
                    steps(pe, step, 2, 3, SEQS)
                    pe.wait_ge(S["sT_done"], 1)
                    for c in range(8):
                        last = pe.transpose(pss[:, c, :], sT[:, c, :], ident[:])
                    last.then_inc(S["s_back"], 1)
                    pe.wait_ge(S["prob_done"], 1)
                    for h in range(HEADS):
                        for m in range(2):
                            last = pe.transpose(psa[:, 2 * h + m, :], prob[:, h, P * m:P * m + P], ident[:])
                    last.then_inc(S["pT_psum"], 1)
                    pe.wait_ge(S["pT_done"], 1)

                    def values(s):
                        pe.wait_ge(kv_here[s.par], 16 * (s.half + 1) + 16 * SEQS // 2)
                        cols = bass.ds(SLEN * s.v, SLEN)
                        for c in range(8):
                            for m in range(2):
                                last = pe.matmul(pso[:, c, cols], kv[s.par][:, m, P * c:P * c + P], pT[:, c // 2 * 2 + m, cols],
                                                 start=(m == 0), stop=(m == 1))
                        last.then_inc(S["o_psum"], 1)
                    steps(pe, values, 2, 3, SEQS)
        q_stack.close()
        kv_stack.close()
        e_stack = ExitStack()
        sbe, _, seme = alloc(e_stack)
        gu_d = (I["w_expert_gate"][0], I["w_expert_up"][0])
        expert_here = [seme(f"expert_here{i}") for i in range(2)]

        def load_expert(eng, e, slot):
            base = experts[:, EXPERT_COLS * slot:EXPERT_COLS * slot + EXPERT_COLS]
            for n, name in enumerate(("w_expert_gate", "w_expert_up")):
                eng.dma_start(base[:, 4096 * n:4096 * n + 4096].rearrange("p (k n) -> p k n", k=KD),
                              I[name][0][bass.ds(e, 1), :, :].rearrange("a (k p) n -> p (a k) n", p=P)).then_inc(expert_here[slot], 16)
            eng.dma_start(base[:, 8192:12288].rearrange("p (k n) -> p k n", k=KE),
                          I["w_expert_down"][0][bass.ds(e, 1), :, :].rearrange("a (k p) n -> p (a k) n", p=P)).then_inc(expert_here[slot], 16)

        with one_stage() as st:
            sb, pb, sem = alloc(st)
            oT = [sb(f"r_oT{i}", [P, 8, P]) for i in range(2)]
            x1 = [sb(f"r_x1{i}", [P, D]) for i in range(2)]
            x2 = [sb(f"r_x2{i}", [P, D]) for i in range(2)]
            h3 = [sb(f"r_h3{i}", [P, D]) for i in range(2)]
            junk = sb("r_junk", [P, D])
            h3T = sb("r_h3T", [P, KD, P])
            gf = sb("r_gffn", [P, D])
            wr = sb("r_w", [P, KD, NG + NE])
            br = sb("r_b", [P, NG + NE])
            ss = sb("r_ss", [P, 2])
            rs = sb("r_rs", [P, 2])
            iota4 = sb("r_iota4", [P, NG])
            iota32 = sb("r_iota32", [P, NE])
            pairs_i = sb("r_pairs", [P, NT, 2], I32)
            lg8 = sb("r_lg8", [P, 8])
            le = sb("r_le", [P, NE])
            gm8 = sb("r_gm8", [P, 8])
            gi8 = sb("r_gi8", [P, 8], U32)
            gif = sb("r_gif", [P, 2])
            ngm = sb("r_ngm", [P, 1])
            eg = sb("r_eg", [P, NG])
            gsum = sb("r_gsum", [P, 1])
            goh = sb("r_goh", [P, NG])
            lsel = sb("r_lsel", [P, EPG, NG])
            le8 = sb("r_le8", [P, EPG])
            v8 = sb("r_v8", [P, 8])
            i8 = sb("r_i8", [P, 8], U32)
            i2f = sb("r_i2f", [P, 2])
            nv1 = sb("r_nv1", [P, 1])
            e2 = sb("r_e2", [P, 1])
            den = sb("r_den", [P, 2])
            ef = [sb(f"r_ef{i}", [P, 2]) for i in range(2)]
            oh = [sb(f"r_oh{i}", [P, 2, NE]) for i in range(2)]
            picked = [sb(f"r_picked{i}", [P, NE]) for i in range(2)]
            rk = sb("r_rk", [P, 2, NE])
            rank = sb("r_rank", [P, 2])
            slotf = sb("r_slotf", [P, 2])
            slot_i = [sb(f"r_slot{i}", [P, 2], I32) for i in range(2)]
            val = [sb(f"r_val{i}", [P, 2], I32) for i in range(2)]
            psx = [pb(f"r_psx{i}", [P, D]) for i in range(2)]
            pst = pb("r_pst", [P, KD, P])
            psr = pb("r_psr", [P, 512])
            psk = pb("r_psk", [P, 512])
            names = ("consts wr_here iotas o_psum x2_done squares eps rstd h3_done turned h3T_done r_psum lg_done gmax gidx gif gexp "
                     "goh lsel le8 v8 i8 i2f ef oh picked gexp2 den gate1 gate2 rank_psum rk rank slotf slot total_done ngm "
                     "nv1 pads rank2").split()
            S = {n: sem("r_" + n) for n in names}
            oT_here = [sem(f"r_oT_here{i}") for i in range(2)]
            x1_here = [sem(f"r_x1_here{i}") for i in range(2)]
            x2_out = [sem(f"r_x2_out{i}") for i in range(2)]
            h3_out = [sem(f"r_h3_out{i}") for i in range(2)]
            scattered = [sem(f"r_scattered{i}") for i in range(2)]
            with nc.Block() as block:
                @block.sync
                def _(sp):
                    def load(t):
                        need(sp, S["o_psum"], t.v - 1)
                        sp.dma_start(oT[t.par][:].rearrange("p c n -> p (c n)"), row(oT_d, t)).then_inc(oT_here[t.par], 16)
                        need(sp, S["x2_done"], t.v - 1)
                        sp.dma_start(x1[t.par][:], row(x1_d, t)).then_inc(x1_here[t.par], 16)

                    def step(s):
                        if isinstance(s.v, int) and s.v == 0:
                            load(s)
                            load(s.at(1))
                            load_expert(sp, 0, 0)
                            load_expert(sp, 1, 1)
                        elif s.at(1).exists():
                            load(s.at(1))
                        sp.wait_ge(S["x2_done"], s.v + 1)
                        sp.dma_start(row(x2_d, s), x2[s.par][:]).then_inc(x2_out[s.par], 16)
                        sp.wait_ge(S["h3_done"], s.v + 1)
                        sp.dma_start(h3_d[bass.ds(P * s.v, P), :], h3[s.par][:]).then_inc(h3_out[s.par], 16)
                    steps(sp, step, 2, 7, NT)
                    for i in range(2):
                        sp.wait_ge(x2_out[i], 16 * (9 - i))
                        sp.wait_ge(h3_out[i], 16 * (9 - i))

                @block.gpsimd
                def _(pool):
                    pool.iota(iota4[:], [[1, NG]], base=0, channel_multiplier=0, allow_small_or_imprecise_dtypes=True).then_inc(S["iotas"], 1)
                    pool.iota(iota32[:], [[1, NE]], base=0, channel_multiplier=0, allow_small_or_imprecise_dtypes=True).then_inc(S["iotas"], 1)
                    pool.iota(pairs_i[:], [[2 * P, NT], [1, 2]], base=0, channel_multiplier=2).then_inc(S["iotas"], 1)

                    def step(s):
                        if s.exists():
                            pool.wait_ge(S["squares"], s.v + 1)
                            need(pool, S["h3_done"], s.v)
                            settle(pool)
                            pool.tensor_scalar(rs[:, 0:1], ss[:, 0:1], EPS, None, ALU.add).then_inc(S["eps"], 1)
                            pool.wait_ge(S["eps"], s.v + 1)
                            pool.tensor_tensor(rs[:, 1:2], rs[:, 0:1], mhalf[:], ALU.pow).then_inc(S["rstd"], 1)
                        t = s.at(-2)
                        if t.exists():
                            pool.wait_ge(S["slot"], t.v + 1)
                            for k in range(2):
                                settle(pool)
                                pool.indirect_dma_start(out=table_d, out_offset=bass.IndirectOffsetOnAxis(ap=slot_i[t.par][:, k:k + 1], axis=0),
                                                        in_=val[t.par][:, k:k + 1], in_offset=None).then_inc(scattered[t.par], 16)
                    steps(pool, step, 2, 7, NT + 2)
                    for i in range(2):
                        pool.wait_ge(scattered[i], 32 * (9 - i))

                @block.scalar
                def _(act):
                    act.dma_start(gf[:], I["g_ffn"].partition_broadcast(P).rearrange("p a d -> p (a d)")).then_inc(S["consts"], 16)
                    act.dma_start(br[:, 0:NG], I["b_router_group"].partition_broadcast(P).rearrange("p a d -> p (a d)")).then_inc(S["consts"], 16)
                    act.dma_start(br[:, NG:NG + NE], I["b_router_expert"].partition_broadcast(P).rearrange("p a g e -> p (a g e)")).then_inc(S["consts"], 16)
                    act.dma_start(wr[:, :, 0:NG], I["w_router_group"][0].rearrange("(k p) g -> p k g", p=P)).then_inc(S["wr_here"], 16)
                    for g in range(NG):
                        act.dma_start(wr[:, :, NG + EPG * g:NG + EPG * g + EPG], I["w_router_expert"][0, g].rearrange("(k p) e -> p k e", p=P)).then_inc(S["wr_here"], 16)

                    def step(s):
                        if s.exists():
                            act.wait_ge(S["x2_done"], s.v + 1)
                            need(act, S["rstd"], s.v)
                            need(act, S["squares"], s.v)
                            act.activation(junk[:], x2[s.par][:], ACT.Square, scale=1 / 32, accum_out=ss[:, 0:1]).then_inc(S["squares"], 1)
                        t = s.at(-1)
                        if t.exists():
                            act.wait_ge(S["turned"], t.v + 1)
                            need(act, S["r_psum"], t.v)
                            act.activation(h3T[:], pst[:], ACT.Copy).then_inc(S["h3T_done"], 1)
                            act.wait_ge(S["ngm"], t.v + 1)
                            need(act, S["gate2"], t.v)
                            act.activation(eg[:], lg8[:, 0:NG], ACT.Exp, bias=ngm[:], accum_out=gsum[:]).then_inc(S["gexp"], 1)
                            act.wait_ge(S["nv1"], t.v + 1)
                            act.activation(e2[:], v8[:, 1:2], ACT.Exp, bias=nv1[:]).then_inc(S["gexp2"], 1)
                    steps(act, step, 2, 7, NT + 1)

                @block.vector
                def _(dve):
                    dve.memset(lg8[:], LOW).then_inc(S["pads"], 1)
                    dve.wait_ge(S["pads"], 1)
                    dve.wait_ge(S["consts"], 48)
                    dve.wait_ge(S["iotas"], 3)

                    def put(ins, name):
                        ins.then_inc(S[name], 1)

                    def route(t):
                        n = t.v + 1
                        dve.wait_ge(S["r_psum"], n)
                        need(dve, S["gexp"], t.v)
                        put(dve.tensor_tensor(lg8[:, 0:NG], psr[:, 0:NG], br[:, 0:NG], ALU.add), "lg_done")
                        put(dve.tensor_tensor(le[:], psr[:, NG:NG + NE], br[:, NG:NG + NE], ALU.add), "lg_done")
                        dve.wait_ge(S["lg_done"], 2 * t.v + 2)
                        settle(dve)
                        put(dve.max(gm8[:], lg8[:]), "gmax")
                        dve.wait_ge(S["gmax"], n)
                        put(dve.tensor_scalar(ngm[:], gm8[:, 0:1], -1.0, None, ALU.mult), "ngm")
                        put(dve.max_index(gi8[:], gm8[:], lg8[:]), "gidx")
                        dve.wait_ge(S["gidx"], n)
                        put(dve.tensor_copy(gif[:, 0:1], gi8[:, 0:1]), "gif")
                        dve.wait_ge(S["gif"], 2 * t.v + 1)
                        put(dve.tensor_scalar(goh[:], iota4[:], gif[:, 0:1], None, ALU.is_equal), "goh")
                        put(dve.tensor_scalar(gif[:, 1:2], gif[:, 0:1], float(EPG), None, ALU.mult), "gif")
                        dve.wait_ge(S["goh"], n)
                        put(dve.tensor_tensor(lsel[:], le[:].rearrange("p (g e) -> p e g", g=NG),
                                              goh[:].unsqueeze(1).to_broadcast([P, EPG, NG]), ALU.mult), "lsel")
                        dve.wait_ge(S["lsel"], n)
                        put(dve.tensor_reduce(le8[:], lsel[:], X, ALU.add), "le8")
                        dve.wait_ge(S["le8"], n)
                        need(dve, S["gexp2"], t.v)
                        settle(dve)
                        put(dve.max(v8[:], le8[:]), "v8")
                        dve.wait_ge(S["v8"], n)
                        put(dve.tensor_scalar(nv1[:], v8[:, 0:1], -1.0, None, ALU.mult), "nv1")
                        put(dve.max_index(i8[:], v8[:], le8[:]), "i8")
                        dve.wait_ge(S["i8"], n)
                        put(dve.tensor_copy(i2f[:], i8[:, 0:2]), "i2f")
                        dve.wait_ge(S["i2f"], n)
                        dve.wait_ge(S["gif"], 2 * t.v + 2)
                        put(dve.tensor_scalar(ef[t.par][:], i2f[:], gif[:, 1:2], None, ALU.add), "ef")
                        dve.wait_ge(S["ef"], n)
                        put(dve.tensor_tensor(oh[t.par][:], iota32[:].unsqueeze(1).to_broadcast([P, 2, NE]),
                                              ef[t.par][:].unsqueeze(2).to_broadcast([P, 2, NE]), ALU.is_equal), "oh")
                        dve.wait_ge(S["oh"], n)
                        put(dve.tensor_tensor(picked[t.par][:], oh[t.par][:, 0, :], oh[t.par][:, 1, :], ALU.add), "picked")
                        dve.wait_ge(S["gexp"], n)
                        dve.wait_ge(S["gexp2"], n)
                        put(dve.tensor_scalar(den[:, 0:1], e2[:], 1.0, gsum[:], ALU.add, ALU.mult), "den")
                        dve.wait_ge(S["den"], n)
                        g = gates[:, bass.ds(t.v, 1), :].rearrange("p a k -> p (a k)")
                        put(dve.reciprocal(g[:, 0:1], den[:, 0:1]), "gate1")
                        dve.wait_ge(S["gate1"], n)
                        put(dve.tensor_tensor(g[:, 1:2], g[:, 0:1], e2[:], ALU.mult), "gate2")

                    def place(t):
                        n = t.v + 1
                        dve.wait_ge(S["rank_psum"], n)
                        dve.wait_ge(S["oh"], n)
                        put(dve.tensor_tensor(rk[:], oh[t.par][:], psk[:, 0:NE].unsqueeze(1).to_broadcast([P, 2, NE]), ALU.mult), "rk")
                        put(dve.tensor_tensor(total[:], total[:], picked[t.par][:], ALU.add), "total_done")
                        dve.wait_ge(S["rk"], n)
                        put(dve.tensor_reduce(rank[:], rk[:], X, ALU.add), "rank")
                        dve.wait_ge(S["rank"], n)
                        put(dve.scalar_tensor_tensor(out=slotf[:], in0=ef[t.par][:], scalar=float(CAP), in1=rank[:], op0=ALU.mult, op1=ALU.add), "slotf")
                        need(dve, scattered[t.par], 32 * t.half)
                        put(dve.tensor_copy(val[t.par][:], pairs_i[:, bass.ds(t.v, 1), :].rearrange("p a k -> p (a k)")), "rank2")
                        dve.wait_ge(S["slotf"], n)
                        dve.wait_ge(S["rank2"], n)
                        put(dve.tensor_copy(slot_i[t.par][:], slotf[:]), "slot")

                    def step(s):
                        if s.exists():
                            dve.wait_ge(S["o_psum"], s.v + 1)
                            dve.wait_ge(x1_here[s.par], 16 * (s.half + 1))
                            need(dve, x2_out[s.par], 16 * s.half)
                            dve.tensor_tensor(x2[s.par][:], psx[s.par][:], x1[s.par][:], ALU.add).then_inc(S["x2_done"], 1)
                        t = s.at(-2)
                        if t.exists():
                            place(t)
                        if s.exists():
                            dve.wait_ge(S["rstd"], s.v + 1)
                            need(dve, h3_out[s.par], 16 * s.half)
                            need(dve, S["turned"], s.v - 1)
                            dve.scalar_tensor_tensor(out=h3[s.par][:], in0=x2[s.par][:], scalar=rs[:, 1:2], in1=gf[:],
                                                     op0=ALU.mult, op1=ALU.mult).then_inc(S["h3_done"], 1)
                        t = s.at(-1)
                        if t.exists():
                            route(t)
                    steps(dve, step, 2, 7, NT + 2)

                @block.tensor
                def _(pe):
                    pe.wait_ge(wxo_here, 16)
                    pe.wait_ge(S["wr_here"], 16 * (NG + 1))

                    def step(s):
                        t = s.at(-1)
                        if t.exists():
                            pe.wait_ge(S["h3_done"], t.v + 1)
                            need(pe, S["h3T_done"], t.v)
                            for k in range(KD):
                                last = pe.transpose(pst[:, k, :], h3[t.par][:, P * k:P * k + P], ident[:])
                            last.then_inc(S["turned"], 1)
                        if s.exists():
                            pe.wait_ge(oT_here[s.par], 16 * (s.half + 1))
                            need(pe, S["x2_done"], s.v - 1)
                            for n in range(2):
                                for k in range(KD):
                                    last = pe.matmul(psx[s.par][:, 512 * n:512 * n + 512], oT[s.par][:, k, :],
                                                     w_xo[:, k, 512 * n:512 * n + 512], start=(k == 0), stop=(k == KD - 1))
                            last.then_inc(S["o_psum"], 1)
                        if t.exists():
                            pe.wait_ge(S["h3T_done"], t.v + 1)
                            need(pe, S["lg_done"], 2 * t.v)
                            for k in range(KD):
                                last = pe.matmul(psr[:, 0:NG + NE], h3T[:, k, :], wr[:, k, :], start=(k == 0), stop=(k == KD - 1))
                            last.then_inc(S["r_psum"], 1)
                        t = s.at(-2)
                        if t.exists():
                            pe.wait_ge(S["picked"], t.v + 1)
                            need(pe, S["total_done"], t.v)
                            need(pe, S["rk"], t.v)
                            pe.matmul(psk[:, 0:NE], lower[:], picked[t.par][:], start=True, stop=False)
                            pe.matmul(psk[:, 0:NE], ones[:], total[:], start=False, stop=True).then_inc(S["rank_psum"], 1)
                    steps(pe, step, 2, 7, NT + 2)
        NB = NBMAX + 4
        slot_of = sbe("slot_of_block", [1, NB], I32)
        expert_of = sbe("expert_of_block", [1, NB], I32)
        ends = sbe("block_ends", [1, NE], I32)
        starts1 = sbe("block_starts1", [1, NE], I32)
        with one_stage() as st:
            sb, pb, sem = alloc(st)
            cnt = sb("p_cnt", [1, NE])
            over = sb("p_over", [1, NE, NT])
            limits = sb("p_limits", [1, NT])
            nblk = sb("p_nblk", [1, NE])
            end = sb("p_end", [1, NE])
            zero = sb("p_zero", [1, NE])
            bidx = sb("p_bidx", [1, NB])
            past = sb("p_past", [1, NB, NE])
            pastn = sb("p_pastn", [1, NB, NE])
            eb = sb("p_eb", [1, NB])
            sbk2 = sb("p_sb", [1, NB])
            tmp = sb("p_tmp", [1, NB])
            sf = sb("p_sf", [1, NE])
            psc = pb("p_psc", [P, 512])
            counted = sem("p_counted")
            link = sem("p_link")
            setup = sem("p_setup")
            with nc.Block() as block:
                @block.tensor
                def _(pe):
                    pe.matmul(psc[:, 0:NE], ones[:], total[:], start=True, stop=True).then_inc(counted, 1)

                @block.gpsimd
                def _(pool):
                    pool.iota(limits[:], [[P, NT]], base=0, channel_multiplier=0, allow_small_or_imprecise_dtypes=True).then_inc(setup, 1)
                    pool.iota(bidx[:], [[1, NB]], base=0, channel_multiplier=0, allow_small_or_imprecise_dtypes=True).then_inc(setup, 1)
                    pool.memset(zero[:], 0.0).then_inc(setup, 1)

                @block.vector
                def _(dve):
                    n = [0]

                    def then(ins):
                        n[0] += 1
                        ins.then_inc(link, 1)
                        dve.wait_ge(link, n[0])
                    dve.wait_ge(setup, 3)
                    dve.wait_ge(counted, 1)
                    then(dve.tensor_copy(cnt[:], psc[0:1, 0:NE]))
                    then(dve.tensor_tensor(over[:], cnt[:].unsqueeze(2).to_broadcast([1, NE, NT]),
                                           limits[:].unsqueeze(1).to_broadcast([1, NE, NT]), ALU.is_gt))
                    then(dve.tensor_reduce(nblk[:], over[:], X, ALU.add))
                    then(dve.tensor_tensor_scan(end[:], nblk[:], zero[:], 0.0, ALU.add, ALU.add))
                    then(dve.tensor_copy(ends[:], end[:]))
                    then(dve.tensor_tensor(sf[:], end[:], nblk[:], ALU.subtract))
                    then(dve.tensor_scalar(sf[:], sf[:], 1.0, None, ALU.add))
                    then(dve.tensor_copy(starts1[:], sf[:]))
                    then(dve.tensor_tensor(past[:], end[:].unsqueeze(1).to_broadcast([1, NB, NE]),
                                           bidx[:].unsqueeze(2).to_broadcast([1, NB, NE]), ALU.is_le))
                    then(dve.tensor_reduce(eb[:], past[:], X, ALU.add))
                    then(dve.tensor_tensor(pastn[:], past[:], nblk[:].unsqueeze(1).to_broadcast([1, NB, NE]), ALU.mult))
                    then(dve.tensor_reduce(sbk2[:], pastn[:], X, ALU.add))
                    then(dve.tensor_tensor(tmp[:], bidx[:], sbk2[:], ALU.subtract))
                    then(dve.tensor_scalar(tmp[:], tmp[:], float(P), None, ALU.mult))
                    then(dve.scalar_tensor_tensor(out=tmp[:], in0=eb[:], scalar=float(CAP), in1=tmp[:], op0=ALU.mult, op1=ALU.add))
                    then(dve.tensor_scalar(tmp[:], tmp[:], float(NE * CAP - P), None, ALU.min))
                    then(dve.tensor_copy(slot_of[:], tmp[:]))
                    then(dve.tensor_scalar(eb[:], eb[:], float(NE - 1), None, ALU.min))
                    then(dve.tensor_copy(expert_of[:], eb[:]))
        with one_stage() as st:
            sb, pb, sem = alloc(st)
            pair = [sb(f"e_pair{i}", [P, 1], I32) for i in range(2)]
            spair = [sb(f"e_spair{i}", [P, 1], I32) for i in range(2)]
            token = [sb(f"e_token{i}", [P, 1], I32) for i in range(2)]
            xg = [sb(f"e_xg{i}", [P, D]) for i in range(2)]
            xT = [sb(f"e_xT{i}", [P, KD, P]) for i in range(2)]
            sg = sb("e_sg", [P, DE])
            hb = sb("e_hb", [P, DE])
            hT = sb("e_hT", [P, KE, P])
            yb = [sb(f"e_y{i}", [P, D]) for i in range(2)]
            psx = pb("e_psx", [P, KD, P])
            psg = pb("e_psg", [P, DE])
            psu = pb("e_psu", [P, DE])
            psh = pb("e_psh", [P, KE, P])
            psy = pb("e_psy", [P, D])
            names = "token_done x_turned xT_done gate_psum up_psum silu_done h_done h_turned hT_done y_psum y_done blocks_left".split()
            S = {n: sem("e_" + n) for n in names}
            pair_here = [sem(f"e_pair_here{i}") for i in range(2)]
            spair_here = [sem(f"e_spair_here{i}") for i in range(2)]
            x_here = [sem(f"e_x_here{i}") for i in range(2)]
            y_out = [sem(f"e_y_out{i}") for i in range(2)]

            def count_blocks(eng):
                return eng.value_load(ends[0:1, NE - 1:NE], min_val=PAIRS // P, max_val=NBMAX)

            def block_steps(eng, nb, parts):
                def step(b):
                    for k, work in parts:
                        t = b.at(k)
                        if isinstance(t.v, int):
                            if 0 <= t.v < PAIRS // P:
                                work(t)
                                continue
                            if t.v < 0:
                                continue
                        with eng.If(t.v < nb):
                            work(t)
                steps(eng, step, 2, (NBMAX - 1) // 2, NBMAX + 1)

            with nc.Block() as block:
                @block.sync
                def _(sp):
                    with sp.Fori(1, NE // 2) as g:
                        for u in range(2):
                            e = 2 * g + u
                            first = sp.value_load(starts1[0:1, bass.ds(e - 1, 1)], min_val=1, max_val=NBMAX + 1)
                            sp.wait_ge(S["blocks_left"], first)
                            load_expert(sp, e, u)

                @block.gpsimd
                def _(pool):
                    nb = count_blocks(pool)

                    def pairs_of(t):
                        base = pool.value_load(slot_of[0:1, bass.ds(t.v, 1)], min_val=0, max_val=NE * CAP - P)
                        return table_d[bass.ds(base, P), :]

                    def fetch(t):
                        src = pairs_of(t)
                        need(pool, S["token_done"], t.v - 1)
                        pool.dma_start(pair[t.par][:], src).then_inc(pair_here[t.par], 16)

                    def fetch_again(t):
                        src = pairs_of(t)
                        need(pool, y_out[t.par], 16 * t.half)
                        pool.dma_start(spair[t.par][:], src).then_inc(spair_here[t.par], 16)

                    def gather(t):
                        pool.wait_ge(S["token_done"], t.v + 1)
                        need(pool, S["x_turned"], t.v - 1)
                        settle(pool)
                        pool.indirect_dma_start(out=xg[t.par][:], out_offset=None, in_=h3_d,
                                                in_offset=bass.IndirectOffsetOnAxis(ap=token[t.par][:], axis=0)).then_inc(x_here[t.par], 16)

                    def scatter(t):
                        pool.wait_ge(S["y_done"], 2 * t.v + 2)
                        pool.wait_ge(spair_here[t.par], 16 * (t.half + 1))
                        need(pool, y_out[1 - t.par], 16 * (t.half + t.par))
                        settle(pool)
                        pool.indirect_dma_start(out=y_d, out_offset=bass.IndirectOffsetOnAxis(ap=spair[t.par][:], axis=0),
                                                in_=yb[t.par][:], in_offset=None).then_inc(y_out[t.par], 16)
                    fetch(fixed(0))
                    fetch(fixed(1))
                    gather(fixed(0))
                    gather(fixed(1))
                    fetch(fixed(2))
                    block_steps(pool, nb, [(2, gather), (3, fetch), (0, fetch_again), (-1, scatter)])
                    for i in range(2):
                        pool.wait_ge(y_out[i], 16 * ((nb + (1 - i)) // 2))

                @block.scalar
                def _(act):
                    nb = count_blocks(act)

                    def silu(t):
                        act.wait_ge(S["gate_psum"], t.v + 1)
                        need(act, S["h_done"], t.v)
                        act.activation(sg[:], psg[:], ACT.Silu).then_inc(S["silu_done"], 1)

                    def hT_out(t):
                        act.wait_ge(S["h_turned"], t.v + 1)
                        act.wait_ge(S["blocks_left"], t.v + 1)
                        act.activation(hT[:], psh[:], ACT.Copy).then_inc(S["hT_done"], 1)

                    def xT_out(t):
                        act.wait_ge(S["x_turned"], t.v + 1)
                        need(act, S["up_psum"], t.v - 1)
                        act.activation(xT[t.par][:, 0:4, :], psx[:, 0:4, :], ACT.Copy).then_inc(S["xT_done"], 1)

                    def y_evac(t):
                        act.wait_ge(S["y_psum"], t.v + 1)
                        need(act, y_out[t.par], 16 * t.half)
                        act.activation(yb[t.par][:, 0:512], psy[:, 0:512], ACT.Copy).then_inc(S["y_done"], 1)
                    xT_out(fixed(0))
                    block_steps(act, nb, [(-1, hT_out), (0, silu), (1, xT_out), (-1, y_evac)])

                @block.vector
                def _(dve):
                    nb = count_blocks(dve)

                    def tokens(t):
                        dve.wait_ge(pair_here[t.par], 16 * (t.half + 1))
                        need(dve, x_here[t.par], 16 * t.half)
                        dve.tensor_scalar(token[t.par][:], pair[t.par][:], 1, None, ALU.arith_shift_right).then_inc(S["token_done"], 1)

                    def xT_out(t):
                        dve.wait_ge(S["x_turned"], t.v + 1)
                        need(dve, S["up_psum"], t.v - 1)
                        dve.tensor_copy(xT[t.par][:, 4:8, :], psx[:, 4:8, :]).then_inc(S["xT_done"], 1)

                    def hidden(t):
                        dve.wait_ge(S["silu_done"], t.v + 1)
                        dve.wait_ge(S["up_psum"], t.v + 1)
                        need(dve, S["h_turned"], t.v)
                        dve.tensor_tensor(hb[:], psu[:], sg[:], ALU.mult).then_inc(S["h_done"], 1)

                    def y_evac(t):
                        dve.wait_ge(S["blocks_left"], t.v + 2)
                        need(dve, y_out[t.par], 16 * t.half)
                        dve.tensor_copy(yb[t.par][:, 512:1024], psy[:, 512:1024]).then_inc(S["y_done"], 1)
                    tokens(fixed(0))
                    tokens(fixed(1))
                    xT_out(fixed(0))
                    block_steps(dve, nb, [(2, tokens), (0, hidden), (1, xT_out), (-1, y_evac)])

                @block.tensor
                def _(pe):
                    nb = count_blocks(pe)
                    pe.sem_inc(S["blocks_left"], 1)

                    def turn_x(t):
                        pe.wait_ge(x_here[t.par], 16 * (t.half + 1))
                        need(pe, S["xT_done"], 2 * t.v)
                        for k in range(KD):
                            last = pe.transpose(psx[:, k, :], xg[t.par][:, P * k:P * k + P], ident[:])
                        last.then_inc(S["x_turned"], 1)

                    def weights(t):
                        e = pe.value_load(expert_of[0:1, bass.ds(t.v, 1)], min_val=0, max_val=NE - 1)
                        return e, (e % 2) * EXPERT_COLS

                    def gate_up(t):
                        e, base = weights(t)
                        for i in range(2):
                            with pe.If((e % 2) == i):
                                pe.wait_ge(expert_here[i], 48 * (e // 2 + 1))
                                pe.nop()
                        pe.wait_ge(S["xT_done"], 2 * t.v + 2)
                        need(pe, S["silu_done"], t.v)
                        for k in range(KD):
                            last = pe.matmul(psg[:], xT[t.par][:, k, :], experts[:, bass.ds(base + 512 * k, 512)], start=(k == 0), stop=(k == KD - 1))
                        last.then_inc(S["gate_psum"], 1)
                        need(pe, S["h_done"], t.v)
                        for k in range(KD):
                            last = pe.matmul(psu[:], xT[t.par][:, k, :], experts[:, bass.ds(base + 4096 + 512 * k, 512)], start=(k == 0), stop=(k == KD - 1))
                        last.then_inc(S["up_psum"], 1)

                    def turn_h(t):
                        pe.wait_ge(S["h_done"], t.v + 1)
                        need(pe, S["hT_done"], t.v)
                        for k in range(KE):
                            last = pe.transpose(psh[:, k, :], hb[:, P * k:P * k + P], ident[:])
                        last.then_inc(S["h_turned"], 1)

                    def down(t):
                        e, base = weights(t)
                        pe.wait_ge(S["hT_done"], t.v + 1)
                        need(pe, S["y_done"], 2 * t.v)
                        for n in range(2):
                            for k in range(KE):
                                last = pe.matmul(psy[:, 512 * n:512 * n + 512], hT[:, k, :],
                                                 experts[:, bass.ds(base + 8192 + 1024 * k + 512 * n, 512)], start=(k == 0), stop=(k == KE - 1))
                            last.then_inc(S["blocks_left" if n else "y_psum"], 1)
                    turn_x(fixed(0))
                    block_steps(pe, nb, [(-1, turn_h), (0, gate_up), (1, turn_x), (-1, down)])
        with one_stage() as st:
            sb, pb, sem = alloc(st)
            x2 = [sb(f"f_x2{i}", [P, D]) for i in range(2)]
            y = [sb(f"f_y{i}", [P, 2, D]) for i in range(2)]
            acc = [sb(f"f_acc{i}", [P, D]) for i in range(2)]
            out = [sb(f"f_out{i}", [P, D]) for i in range(2)]
            gl = sb("f_gfinal", [P, D])
            junk = sb("f_junk", [P, D])
            ss = sb("f_ss", [P, 2])
            rs = sb("f_rs", [P, 4])
            S = {n: sem("f_" + n) for n in "gl_here first second squares eps rstd out_done".split()}
            x2_here = [sem(f"f_x2_here{i}") for i in range(2)]
            y_here = [sem(f"f_y_here{i}") for i in range(2)]
            out_sent = [sem(f"f_out_sent{i}") for i in range(2)]
            y_p = O["y_p"].rearrange("b (t p) d -> (b t) p d", p=P)
            y_pairs = y_d[0:PAIRS, :].rearrange("(t p k) d -> t p k d", p=P, k=2)
            with nc.Block() as block:
                @block.sync
                def _(sp):
                    def step(s):
                        if s.exists():
                            need(sp, S["second"], s.v - 1)
                            sp.dma_start(x2[s.par][:], row(x2_d, s)).then_inc(x2_here[s.par], 16)
                            sp.dma_start(y[s.par][:], y_pairs[bass.ds(s.v, 1), :, :, :].rearrange("a p k d -> (a p) k d")).then_inc(y_here[s.par], 16)
                    steps(sp, step, 2, 7, NT)

                @block.gpsimd
                def _(pool):
                    def step(t):
                        pool.wait_ge(S["squares"], t.v + 1)
                        need(pool, S["out_done"], t.v)
                        settle(pool)
                        pool.tensor_scalar(rs[:, 0:1], ss[:, 0:1], EPS, None, ALU.add).then_inc(S["eps"], 1)
                        pool.wait_ge(S["eps"], t.v + 1)
                        pool.tensor_tensor(rs[:, 1:2], rs[:, 0:1], mhalf[:], ALU.pow).then_inc(S["rstd"], 1)
                    steps(pool, step, 2, 7, NT)

                @block.scalar
                def _(act):
                    act.dma_start(gl[:], I["g_final"].rearrange("(a d) -> a d", a=1).partition_broadcast(P).rearrange("p a d -> p (a d)")).then_inc(S["gl_here"], 16)

                    def store(t):
                        act.wait_ge(S["out_done"], t.v + 1)
                        dst = O["y_s"].rearrange("b t d -> (b t) d") if isinstance(t.v, int) and t.v == PT else \
                            y_p[bass.ds(t.v, 1), :, :].rearrange("a p d -> (a p) d")
                        act.dma_start(dst, out[t.par][:]).then_inc(out_sent[t.par], 16)

                    def step(s):
                        if s.exists():
                            act.wait_ge(S["second"], s.v + 1)
                            need(act, S["rstd"], s.v)
                            need(act, S["squares"], s.v)
                            act.activation(junk[:], acc[s.par][:], ACT.Square, scale=1 / 32, accum_out=ss[:, 0:1]).then_inc(S["squares"], 1)
                        if s.at(-1).exists():
                            store(s.at(-1))
                    steps(act, step, 2, 7, NT + 1)
                    act.wait_ge(out_sent[0], 16 * 9)
                    act.wait_ge(out_sent[1], 16 * 8)

                @block.vector
                def _(dve):
                    dve.wait_ge(S["gl_here"], 16)

                    def step(s):
                        g = gates[:, bass.ds(s.v, 1), :].rearrange("p a k -> p (a k)") if s.exists() else None
                        if s.exists():
                            dve.wait_ge(x2_here[s.par], 16 * (s.half + 1))
                            dve.wait_ge(y_here[s.par], 16 * (s.half + 1))
                            need(dve, S["out_done"], s.v - 1)
                            dve.scalar_tensor_tensor(out=acc[s.par][:], in0=y[s.par][:, 0, :], scalar=g[:, 0:1], in1=x2[s.par][:],
                                                     op0=ALU.mult, op1=ALU.add).then_inc(S["first"], 1)
                            dve.wait_ge(S["first"], s.v + 1)
                            dve.scalar_tensor_tensor(out=acc[s.par][:], in0=y[s.par][:, 1, :], scalar=g[:, 1:2], in1=acc[s.par][:],
                                                     op0=ALU.mult, op1=ALU.add).then_inc(S["second"], 1)
                        t = s.at(-1)
                        if t.exists():
                            dve.wait_ge(S["rstd"], t.v + 1)
                            need(dve, out_sent[t.par], 16 * t.half)
                            dve.scalar_tensor_tensor(out=out[t.par][:], in0=acc[t.par][:], scalar=rs[:, 1:2], in1=gl[:],
                                                     op0=ALU.mult, op1=ALU.mult).then_inc(S["out_done"], 1)
                    steps(dve, step, 2, 7, NT + 1)
        e_stack.close()


_INS = ["x_prompt", "x_sample", "mem_prompt", "state_conv", "cache_mem_k", "cache_mem_v", "g_mix", "w_in", "conv_w", "conv_b",
        "ln_conv_g", "ln_conv_b", "ln_v_g", "ln_v_b", "w_sg", "b_sg", "w_out", "g_mem", "w_mk", "w_mv", "g_xattn", "w_xq",
        "w_xo", "g_ffn", "w_router_group", "b_router_group", "w_router_expert", "b_router_expert", "w_expert_gate",
        "w_expert_up", "w_expert_down", "g_final"]
_OUTS = {"y_p": (1, 2048, D), "y_s": (SEQS, SLEN, D), "state_p": (HIST, DC), "state_s": (SEQS, HIST, DC),
         "k": (NMEM, D), "v": (NMEM, D), "sgv": (P, DC)}


def kernel(**inputs):
    import concourse.bacc as bacc
    from concourse.bass_utils import run_bass_kernel_spmd

    nc = bacc.Bacc("TRN2", target_bir_lowering=False, num_devices=1)
    arrays, I, O = {}, {}, {}
    for name in _INS:
        a = np.ascontiguousarray(inputs[name])
        arrays[f"in_{name}"] = a
        I[name] = nc.dram_tensor(f"in_{name}", a.shape, mybir.dt.from_np(a.dtype), kind="ExternalInput").ap()
    for name, shape in _OUTS.items():
        O[name] = nc.dram_tensor(f"out_{name}", shape, F32, kind="ExternalOutput").ap()
    build(nc, I, O)
    r = run_bass_kernel_spmd(nc, [arrays], core_ids=[0]).results[0]
    return (r["out_y_p"], r["out_y_s"], r["out_state_p"].reshape(1, 1, HIST, DC), r["out_state_s"].reshape(1, SEQS, HIST, DC),
            r["out_k"].reshape(1, 1, NMEM, HEADS, HD), r["out_v"].reshape(1, 1, NMEM, HEADS, HD),
            r["out_sgv"].reshape(1, SEQS, SLEN, DC))
```

```python
from contextlib import ExitStack, contextmanager

import numpy as np
import concourse.bass as bass
from concourse import mybir

F32 = mybir.dt.float32
I32 = mybir.dt.int32
U32 = mybir.dt.uint32
ALU = mybir.AluOpType
ACT = mybir.ActivationFunctionType
X = mybir.AxisListType.X

P = 128
D = 1024
KD = D // P
NT = 17
PT = 16
SEQS, SLEN = 8, 16
DC = 512
CG = DC // P
TAPS = 31
HIST = TAPS - 1
HEADS, HD = 4, 256
NMEM = 256
SCALE = HD ** -0.5
NG, EPG, NE = 4, 8, 32
DE = 512
KE = DE // P
TOK = NT * P
PAIRS = 2 * TOK
CAP = TOK
NBMAX = (PAIRS - NE) // P + NE
EXPERT_COLS = 3 * 4096
SLOTS = 3
EPS = 1e-6
LOW = -3.0e38


class Tile:

    def __init__(self, v, half, par):
        self.v, self.half, self.par = v, half, par

    def at(self, k):
        par = (self.par + k) % 2
        return Tile(self.v + k, self.half + (self.par + k - par) // 2, par)

    def exists(self, n=NT):
        return not isinstance(self.v, int) or 0 <= self.v < n


def fixed(v):
    return Tile(v, v // 2, v % 2)


def need(eng, sem, value):
    if isinstance(value, int) and value <= 0:
        return
    eng.wait_ge(sem, value)


def steps(eng, step, first, pairs, total):
    for s in range(first):
        step(fixed(s))
    if pairs:
        with eng.Fori(0, pairs) as g:
            for u in range(2):
                step(Tile(2 * g + (first + u), g + first // 2, u))
    for s in range(first + 2 * pairs, total):
        step(fixed(s))


def build(nc, I, O):
    top = ExitStack()
    stages, stage_sems = [], []

    @contextmanager
    def one_stage():
        with ExitStack() as st:
            stages.append(st)
            yield st
            numbers = sorted(handle.num for handle in stage_sems)
            while numbers:
                n = 1
                while n < len(numbers) and numbers[n] == numbers[0] + n:
                    n += 1
                nc.gpsimd.sem_clear(range(numbers[0], numbers[0] + n))
                numbers = numbers[n:]
            stage_sems.clear()
            nc.all_engine_barrier()

    with top:
        def alloc(stack):
            def sb(name, shape, dt=F32):
                return stack.enter_context(nc.sbuf_tensor(name, shape, dt))

            def pb(name, shape, dt=F32):
                return stack.enter_context(nc.psum_tensor(name, shape, dt))

            def sem(name):
                handle = stack.enter_context(nc.semaphore(name))
                if stack in stages:
                    stage_sems.append(handle)
                return handle
            return sb, pb, sem

        sb, _, sem = alloc(top)
        mixb_d = nc.dram_tensor("mixb_scratch", [NT, P, DC], F32, kind="Internal").ap()
        x1_d = nc.dram_tensor("x1_scratch", [NT, P, D], F32, kind="Internal").ap()
        oT_d = nc.dram_tensor("oT_scratch", [NT, P, D], F32, kind="Internal").ap()
        x2_d = nc.dram_tensor("x2_scratch", [NT, P, D], F32, kind="Internal").ap()
        h3_d = nc.dram_tensor("h3_scratch", [TOK + P // 2, D], F32, kind="Internal").ap()
        y_d = nc.dram_tensor("y_scratch", [PAIRS + P, D], F32, kind="Internal").ap()
        table_d = nc.dram_tensor("table_scratch", [NE * CAP, 1], I32, kind="Internal").ap()

        ident = sb("ident", [P, P])
        ones = sb("ones", [P, P])
        mhalf = sb("mhalf", [P, 1])
        gcol = sb("gcol", [P, 3 * KD])
        pcol = sb("pcol", [P, CG, 34])
        gates = sb("gates", [P, NT, 2])
        total = sb("total", [P, NE])
        wr = sb("router_w", [P, KD, NG + NE])
        br = sb("router_b", [P, NG + NE])
        W = sb("W", [P, SLOTS * EXPERT_COLS])
        w_in = W[:, 0:16384].rearrange("p (k n) -> p k n", k=KD)
        w_out = W[:, 16384:24576].rearrange("p (k n) -> p k n", k=KD)
        w_xq = W[:, 8192:16384].rearrange("p (k n) -> p k n", k=KD)
        w_xo = W[:, 0:8192].rearrange("p (k n) -> p k n", k=KD)
        w_mk = W[:, 16384:24576].rearrange("p (k n) -> p k n", k=KD)
        w_mv = W[:, 24576:32768].rearrange("p (k n) -> p k n", k=KD)
        spare = [W[:, 32768 + D * i:32768 + D * i + D] for i in range(4)]
        settled = {nc.sync: sem("settled_sync"), nc.vector: sem("settled_vector"), nc.gpsimd: sem("settled_pool")}

        def settle(eng):
            eng.sem_inc(settled[eng], 1)

        win_here = sem("win_here")
        wout_here = sem("wout_here")
        wxq_here = sem("wxq_here")
        wxo_here = sem("wxo_here")
        wr_here = sem("wr_here")
        only_zero = sem("only_zero")
        kv_stack = ExitStack()
        sbk, _, _ = alloc(kv_stack)
        KT = sbk("KT", [P, 8, NMEM])
        V = sbk("V", [P, 2, D])
        mix_stack = ExitStack()
        sbm, _, _ = alloc(mix_stack)
        sgT = sbm("sgT", [P, HEADS, P])
        sgT_s = sbm("sgT_s", [P, HEADS, P])
        bsg = sbm("bsg", [P, HEADS])
        bsg_s = sbm("bsg_s", [P, HEADS])
        sext = sbm("sext", [P, CG, SEQS, HIST + SLEN])

        x_p = I["x_prompt"].rearrange("b (t p) d -> (b t) p d", p=P)
        x_s = I["x_sample"].rearrange("b t d -> (b t) d")
        kview = "(k p) n -> p k n"

        def load_x(sp, dst, t):
            if isinstance(t.v, int) and t.v == PT:
                return sp.dma_start(dst, x_s)
            return sp.dma_start(dst, x_p[bass.ds(t.v, 1), :, :].rearrange("a p d -> (a p) d"))

        def row(dram, t):
            return dram[bass.ds(t.v, 1), :, :].rearrange("a p d -> (a p) d")

        with one_stage() as st:
            sb, pb, sem = alloc(st)
            mem = W[:, 32768:32768 + 2 * D].rearrange("p (m d) -> p m d", m=2)
            memn = sb("memn", [P, D])
            memT = W[:, 32768 + 2 * D:32768 + 4 * D].rearrange("p (k n) -> p k n", k=KD)
            junk = memn
            K = mem
            ss = sb("m_ss", [P, 2])
            rstd = sb("m_rstd", [P, 2])
            sgw = sb("sgw", [P, HEADS, P])
            sgw_s = sb("sgw_s", [P, HEADS, P])
            grow = sb("grow", [3 * KD, P])
            prow = sb("prow", [34, DC])
            hrow = sb("hrow", [120, 2, DC])
            pst = [pb(f"m_pst{i}", [P, 8, P]) for i in range(1)]
            psc = [pb(f"m_psc{i}", [P, 4, P]) for i in range(2)]
            psk = [pb(f"m_psk{i}", [P, 512]) for i in range(4)]
            mem_here = sem("mem_here")
            grow_here = sem("grow_here")
            small_here = sem("small_here")
            sg_here = sem("sg_here")
            blocks_here = sem("blocks_here")
            wmk_here = sem("wmk_here")
            wmv_here = sem("wmv_here")
            ident_set = sem("ident_set")
            ident_done = sem("ident_done")
            sgs_zero = sem("sgs_zero")
            sg_masked = sem("sg_masked")
            squares = sem("m_squares")
            eps_added = sem("m_eps")
            rstd_done = sem("m_rstd_done")
            normed = sem("m_normed")
            turned = sem("m_turned")
            memT_done = sem("memT_done")
            kv_psum = sem("kv_psum")
            kv_sbuf = sem("kv_sbuf")
            kt_psum = sem("kt_psum")
            kt_done = sem("kt_done")
            kv_out = sem("kv_out")
            const_psum = sem("const_psum")
            const_done = sem("const_done")
            table_set = sem("table_set")
            table_sent = sem("table_sent")
            hist_out = sem("hist_out")
            tabf = sb("tabf", [P, NE * CAP // P], I32)
            tabm = sb("tabm", [P, NE * CAP // P], I32)
            zrow = sb("zrow", [P // 2, D])
            with nc.Block() as block:
                @block.sync
                def _(sp):
                    sp.dma_start(mem[:], I["mem_prompt"].rearrange("b (m p) d -> p (b m) d", p=P)).then_inc(mem_here, 16)
                    sp.wait_ge(mem_here, 16)
                    sp.dma_start(w_mk, I["w_mk"][0].rearrange(kview, p=P)).then_inc(wmk_here, 16)
                    sp.wait_ge(wmk_here, 16)
                    sp.dma_start(w_mv, I["w_mv"][0].rearrange(kview, p=P)).then_inc(wmv_here, 16)
                    sp.wait_ge(wmv_here, 16)
                    for n in range(4):
                        sp.dma_start(w_in[:, :, 512 * n:512 * n + 512],
                                     I["w_in"][0][:, 512 * n:512 * n + 512].rearrange(kview, p=P)).then_inc(win_here, 16)
                    for n in range(4):
                        sp.wait_ge(kv_sbuf, n + 1)
                        sp.dma_start(O["k"][P * (n // 2):P * (n // 2) + P, 512 * (n % 2):512 * (n % 2) + 512],
                                     K[:, n // 2, 512 * (n % 2):512 * (n % 2) + 512]).then_inc(kv_out, 16)
                    for n in range(4):
                        sp.wait_ge(kv_sbuf, n + 5)
                        sp.dma_start(O["v"][P * (n // 2):P * (n // 2) + P, 512 * (n % 2):512 * (n % 2) + 512],
                                     V[:, n // 2, 512 * (n % 2):512 * (n % 2) + 512]).then_inc(kv_out, 16)
                    sp.wait_ge(table_set, 4)
                    sp.dma_start(table_d.rearrange("(p q) a -> p (q a)", p=P), tabf[:]).then_inc(table_sent, 16)
                    sp.dma_start(h3_d[TOK:TOK + P // 2, :], zrow[:]).then_inc(table_sent, 16)
                    sp.wait_ge(kv_out, 128)
                    sp.wait_ge(table_sent, 32)

                @block.gpsimd
                def _(pool):
                    pool.memset(ident[:], 0.0).then_inc(ident_set, 1)
                    pool.memset(mhalf[:], -0.5).then_inc(ident_set, 1)
                    pool.memset(ones[:], 1.0).then_inc(ident_set, 1)
                    pool.memset(total[:], 0.0).then_inc(ident_set, 1)
                    pool.memset(zrow[:], 0.0).then_inc(table_set, 1)
                    pool.memset(sgw_s[:], 0.0).then_inc(sgs_zero, 1)
                    pool.iota(tabm[:], [[1, NE * CAP // P]], base=0, channel_multiplier=NE * CAP // P).then_inc(table_set, 1)
                    pool.wait_ge(ident_set, 4)
                    pool.affine_select(out=ident[:], in_=ident[:], compare_op=ALU.not_equal, fill=1.0, base=0,
                                       pattern=[[-1, P]], channel_multiplier=1).then_inc(ident_done, 1)
                    for m in range(2):
                        pool.wait_ge(squares, m + 1)
                        settle(pool)
                        pool.tensor_scalar(rstd[:, m:m + 1], ss[:, m:m + 1], EPS, None, ALU.add).then_inc(eps_added, 1)
                        pool.wait_ge(eps_added, m + 1)
                        pool.tensor_tensor(rstd[:, m:m + 1], rstd[:, m:m + 1], mhalf[:], ALU.pow).then_inc(rstd_done, 1)
                    for n, (w, ready) in enumerate(((sgw, sg_here), (sgw_s, blocks_here))):
                        pool.wait_ge(ready, 16 * (1 if n == 0 else SEQS))
                        pool.affine_select(out=w[:], in_=w[:], compare_op=ALU.is_ge, fill=0.0, base=0,
                                           pattern=[[0, HEADS], [-1, P]], channel_multiplier=1).then_inc(sg_masked, 1)

                @block.scalar
                def _(act):
                    act.dma_start(grow[0:8, :], I["g_mix"][0].rearrange("(k p) -> k p", p=P)).then_inc(grow_here, 16)
                    act.dma_start(grow[8:16, :], I["g_xattn"][0].rearrange("(k p) -> k p", p=P)).then_inc(grow_here, 16)
                    act.dma_start(grow[16:24, :], I["g_mem"][0].rearrange("(k p) -> k p", p=P)).then_inc(grow_here, 16)
                    act.dma_start(prow[0:31, :], I["conv_w"][0]).then_inc(small_here, 16)
                    act.dma_start(prow[31:32, :], I["conv_b"]).then_inc(small_here, 16)
                    act.dma_start(prow[32:33, :], I["ln_conv_g"]).then_inc(small_here, 16)
                    act.dma_start(prow[33:34, :], I["ln_conv_b"]).then_inc(small_here, 16)
                    act.dma_start(hrow[:], I["state_conv"][0].rearrange("(a b) r c -> (b r) a c", a=2)).then_inc(small_here, 16)
                    act.dma_start(sgw[:], I["w_sg"][0].rearrange("h i j -> i h j")).then_inc(sg_here, 16)
                    act.wait_ge(sgs_zero, 1)
                    for s in range(SEQS):
                        r = slice(SLEN * s, SLEN * s + SLEN)
                        act.dma_start(sgw_s[r, :, r], I["w_sg"][0][:, 0:SLEN, 0:SLEN].rearrange("h i j -> i h j")).then_inc(blocks_here, 16)
                    act.dma_start(bsg[:], I["b_sg"][0].rearrange("h i -> i h"), allow_slow_non_contiguous=True).then_inc(small_here, 16)
                    for s in range(SEQS):
                        act.dma_start(bsg_s[SLEN * s:SLEN * s + SLEN, :], I["b_sg"][0][:, 0:SLEN].rearrange("h i -> i h"),
                                      allow_slow_non_contiguous=True).then_inc(small_here, 16)
                    act.dma_start(O["state_s"][:, 0:HIST - SLEN, :], I["state_conv"][0][:, SLEN:HIST, :]).then_inc(hist_out, 16)
                    act.wait_ge(mem_here, 16)
                    for m in range(2):
                        if m:
                            act.wait_ge(turned, 8)
                        act.activation(junk[:], mem[:, m, :], ACT.Square, scale=1 / 32, accum_out=ss[:, m:m + 1]).then_inc(squares, 1)
                        act.wait_ge(rstd_done, m + 1)
                        act.wait_ge(squares, m + 1)
                        act.activation(memn[:], mem[:, m, :], ACT.Copy, scale=rstd[:, m:m + 1]).then_inc(normed, 1)
                        act.wait_ge(const_done, 1)
                        act.wait_ge(turned, 8 * (m + 1))
                        for k in range(KD):
                            act.activation(memT[:, k, P * m:P * m + P], pst[0][:, k, :], ACT.Copy,
                                           scale=gcol[:, 16 + k:17 + k]).then_inc(memT_done, 1)
                    act.wait_ge(hist_out, 16)
                    act.wait_ge(small_here, 16 * 14)

                @block.vector
                def _(dve):
                    dve.wait_ge(table_set, 2)
                    dve.tensor_scalar(tabm[:], tabm[:], P - 1, None, ALU.bitwise_and).then_inc(table_set, 1)
                    dve.wait_ge(table_set, 3)
                    dve.tensor_scalar(tabf[:], tabm[:], float(PAIRS), None, ALU.add).then_inc(table_set, 1)
                    dve.wait_ge(const_psum, 1)
                    dve.tensor_copy(gcol[:], psc[0][:, 0, 0:3 * KD]).then_inc(const_done, 1)
                    for n in range(8):
                        dst = (K if n < 4 else V)[:, n % 4 // 2, 512 * (n % 2):512 * (n % 2) + 512]
                        dve.wait_ge(kv_psum, n + 1)
                        dve.tensor_copy(dst, psk[n % 4][:]).then_inc(kv_sbuf, 1)
                    for n in range(4):
                        dve.wait_ge(kt_psum, n + 1)
                        dve.tensor_copy(KT[:, 4 * (n // 2):4 * (n // 2) + 4, P * (n % 2):P * (n % 2) + P], psk[n][:].rearrange("p (k m) -> p k m", k=4)).then_inc(kt_done, 1)
                    dve.wait_ge(const_psum, 2)
                    dve.tensor_copy(pcol[:], psc[1][:, :, 0:34]).then_inc(const_done, 1)
                    for a in range(2):
                        dve.wait_ge(const_psum, 3 + a)
                        dve.tensor_copy(sext[:, :, 4 * a:4 * a + 4, 0:HIST],
                                        psc[a][:, :, 0:120].rearrange("p c (s r) -> p c s r", r=HIST)).then_inc(const_done, 1)
                    dve.wait_ge(const_psum, 5)
                    dve.tensor_copy(sgT[:], psc[0][:]).then_inc(const_done, 1)
                    dve.wait_ge(const_psum, 6)
                    dve.tensor_copy(sgT_s[:], psc[1][:]).then_inc(const_done, 1)

                @block.tensor
                def _(pe):
                    pe.wait_ge(ident_done, 1)
                    pe.wait_ge(grow_here, 48)
                    pe.transpose(psc[0][:, 0, 0:3 * KD], grow[:], ident[0:3 * KD, 0:3 * KD]).then_inc(const_psum, 1)
                    for m in range(2):
                        pe.wait_ge(normed, m + 1)
                        if m:
                            pe.wait_ge(memT_done, KD)
                        for k in range(KD):
                            pe.transpose(pst[0][:, k, :], memn[:, P * k:P * k + P], ident[:]).then_inc(turned, 1)
                    pe.wait_ge(memT_done, 2 * KD)
                    for n in range(8):
                        w = w_mk if n < 4 else w_mv
                        if n % 4 == 0:
                            pe.wait_ge(wmk_here if n < 4 else wmv_here, 16)
                        if n >= 4:
                            pe.wait_ge(kv_sbuf, n - 3)
                        m, c = n % 4 // 2, 512 * (n % 2)
                        for k in range(KD):
                            last = pe.matmul(psk[n % 4][:], memT[:, k, P * m:P * m + P], w[:, k, c:c + 512],
                                             start=(k == 0), stop=(k == KD - 1))
                        last.then_inc(kv_psum, 1)
                    for n in range(4):
                        pe.wait_ge(kv_sbuf, n + 5)
                        for j in range(4):
                            k = 4 * (n // 2) + j
                            last = pe.transpose(psk[n][:, P * j:P * j + P], K[:, n % 2, P * k:P * k + P], ident[:])
                        last.then_inc(kt_psum, 1)
                    pe.wait_ge(small_here, 16 * 14)
                    for c in range(CG):
                        last = pe.transpose(psc[1][:, c, 0:34], prow[:, P * c:P * c + P], ident[0:34, 0:34])
                    last.then_inc(const_psum, 1)
                    for a in range(2):
                        pe.wait_ge(const_done, 1 + a)
                        for c in range(CG):
                            last = pe.transpose(psc[a][:, c, 0:120], hrow[:, a, P * c:P * c + P], ident[0:120, 0:120])
                        last.then_inc(const_psum, 1)
                    for a, w in enumerate((sgw, sgw_s)):
                        pe.wait_ge(const_done, 3 + a)
                        pe.wait_ge(sg_masked, a + 1)
                        for h in range(HEADS):
                            last = pe.transpose(psc[a][:, h, :], w[:, h, :], ident[:])
                        last.then_inc(const_psum, 1)

        with one_stage() as st:
            sb, pb, sem = alloc(st)
            x_in = [spare[0]]
            xn = x_in[0]
            mbl = [W[:, 24576 + DC * i:24576 + DC * (i + 1)].rearrange("p (c n) -> p c n", c=CG) for i in range(2)]
            x1 = [W[:, 24576 + D * (1 + i):24576 + D * (2 + i)] for i in range(2)]
            mixed = W[:, 24576 + 3 * D:24576 + 4 * D]
            hT = [spare[1 + i].rearrange("p (k n) -> p k n", k=KD) for i in range(2)]
            junk = spare[3]
            sig = sb("a_sig", [P, DC])
            a_tok = [sb(f"a_tok{i}", [P, DC]) for i in range(2)]
            stage = [sb(f"a_stage{i}", [P, CG, P]) for i in range(2)]
            aext = sb("aext", [P, CG, HIST + 2 * P])
            yacc = sb("yacc", [P, 2, 2 * P])
            ybuf = sb("ybuf", [P, CG, 2 * P])
            u_sb = sb("a_u", [P, DC])
            vn = sb("a_vn", [P, DC])
            b_tok = sb("a_btok", [P, DC])
            maT = sb("a_maT", [P, CG, P])
            mbT = sb("a_mbT", [P, CG, P])
            gv = sb("gv", [P, DC])
            bv = sb("bv", [P, DC])
            ss = sb("a_ss", [P, 2])
            rs = sb("a_rs", [P, 2])
            vst = sb("a_vst", [P, 6])
            vmv = sb("a_vmv", [P, 2])
            vrs = sb("a_vrs", [P, 2])
            yst = sb("a_yst", [P, 6])
            ymv = sb("a_ymv", [P, 2])
            yrs = sb("a_yrs", [P, 2])
            yn = junk[:, 0:DC]
            psz = [pb(f"a_psz{i}", [P, 512]) for i in range(4)]
            pst = pb("a_pst", [P, 4, P])
            psx = pb("a_psx", [P, CG, P])
            psg = pb("a_psg", [P, HEADS, P])
            psy = pb("a_psy", [P, CG, P])
            names = ("x_here0 v_consts squares eps rstd normed turned hT_done gate_psum val_psum v_psum u_psum tanh_done "
                     "sig_done a_done aT_psum stage_full ext_ready conv_step y_ready vstat vagg veps vrstd vnmr vnormed "
                     "vgain v_done sg_psum u_done b_done bT_psum mb_done mb_out yT_psum ystat yagg yeps yrstd ynmr "
                     "ynormed ynT_psum ma_done state_out halo wo_psum wo_read x1_half").split()
            S = {n: sem("a_" + n) for n in names}
            mbl_here = [sem(f"a_mbl_here{i}") for i in range(2)]
            x1_in = [sem(f"a_x1_in{i}") for i in range(2)]
            x1_out = [sem(f"a_x1_out{i}") for i in range(2)]
            GATE, VAL, VV, UU = range(4)
            COL = [512, 0, 1536, 1024]

            with nc.Block() as block:
                @block.sync
                def _(sp):
                    sp.dma_start(gv[:], I["ln_v_g"].partition_broadcast(P).rearrange("p a d -> p (a d)")).then_inc(S["v_consts"], 16)
                    sp.dma_start(bv[:], I["ln_v_b"].partition_broadcast(P).rearrange("p a d -> p (a d)")).then_inc(S["v_consts"], 16)

                    def load(t):
                        need(sp, S["turned"], 2 * t.v)
                        settle(sp)
                        load_x(sp, x_in[0][:], t).then_inc(S["x_here0"], 16)

                    def store_b(t):
                        sp.wait_ge(S["mb_done"], t.v + 1)
                        sp.dma_start(row(mixb_d, t), mbT[:].rearrange("p c n -> p (c n)")).then_inc(S["mb_out"], 16)

                    def load_b(t):
                        sp.wait_ge(S["mb_out"], 16 * (t.v + 1))
                        settle(sp)
                        need(sp, S["wo_psum"], 2 * (t.v - 1))
                        settle(sp)
                        sp.dma_start(mbl[t.par].rearrange("p c n -> p (c n)"), row(mixb_d, t)).then_inc(mbl_here[t.par], 16)
                        need(sp, x1_out[t.par], 16 * t.half)
                        settle(sp)
                        load_x(sp, x1[t.par], t).then_inc(x1_in[t.par], 16)

                    def store_x1(t):
                        sp.wait_ge(S["x1_half"], 2 * t.v + 2)
                        settle(sp)
                        sp.dma_start(row(x1_d, t), x1[t.par]).then_inc(x1_out[t.par], 16)

                    def step(s):
                        if s.exists() and isinstance(s.v, int) and s.v == 0:
                            load(s)
                        if s.at(1).exists():
                            load(s.at(1))
                        if isinstance(s.v, int) and s.v == 1:
                            sp.dma_start(w_out, I["w_out"][0].rearrange(kview, p=P)).then_inc(wout_here, 16)
                        if isinstance(s.v, int) and s.v == NT:
                            sp.wait_ge(S["u_psum"], NT)
                            sp.dma_start(w_xq, I["w_xq"][0].rearrange(kview, p=P)).then_inc(wxq_here, 16)
                            sp.dma_start(w_xo, I["w_xo"][0].rearrange(kview, p=P)).then_inc(wxo_here, 16)
                        if s.at(-3).exists():
                            load_b(s.at(-3))
                        if s.at(-1).exists():
                            store_b(s.at(-1))
                        if isinstance(s.v, int) and s.v == PT - 1:
                            sp.wait_ge(S["a_done"], PT)
                            sp.dma_start(O["state_p"], a_tok[1][P - HIST:P, :]).then_inc(S["state_out"], 16)
                        if isinstance(s.v, int) and s.v == PT:
                            sp.wait_ge(S["a_done"], NT)
                            for q in range(SEQS):
                                sp.dma_start(O["state_s"][q, HIST - SLEN:HIST, :], a_tok[0][SLEN * q:SLEN * q + SLEN, :]).then_inc(S["state_out"], 16)
                            sp.wait_ge(S["v_done"], NT)
                            sp.dma_start(O["sgv"], vn[:]).then_inc(S["state_out"], 16)
                        if s.at(-4).exists():
                            store_x1(s.at(-4))
                    steps(sp, step, 6, 4, 21)
                    sp.wait_ge(S["state_out"], 16 * 10)
                    for i in range(2):
                        sp.wait_ge(x1_out[i], 16 * (9 - i))
                    sp.wait_ge(S["mb_out"], 16 * NT)

                @block.gpsimd
                def _(pool):
                    def rms(t):
                        pool.wait_ge(S["squares"], t.v + 1)
                        settle(pool)
                        pool.tensor_scalar(rs[:, t.par:t.par + 1], ss[:, t.par:t.par + 1], EPS, None, ALU.add).then_inc(S["eps"], 1)
                        pool.wait_ge(S["eps"], t.v + 1)
                        pool.tensor_tensor(rs[:, t.par:t.par + 1], rs[:, t.par:t.par + 1], mhalf[:], ALU.pow).then_inc(S["rstd"], 1)

                    def norm_consts(t, mv, r, stat, used, eps, rstd, nmr):
                        need(pool, S[used], t.v)
                        pool.wait_ge(S[stat], t.v + 1)
                        settle(pool)
                        pool.tensor_scalar(r[:, 0:1], mv[:, 1:2], EPS, None, ALU.add).then_inc(S[eps], 1)
                        pool.wait_ge(S[eps], t.v + 1)
                        pool.tensor_tensor(r[:, 0:1], r[:, 0:1], mhalf[:], ALU.pow).then_inc(S[rstd], 1)
                        pool.wait_ge(S[rstd], t.v + 1)
                        settle(pool)
                        pool.tensor_scalar(r[:, 1:2], mv[:, 0:1], r[:, 0:1], -1.0, ALU.mult, ALU.mult).then_inc(S[nmr], 1)

                    def step(s):
                        if isinstance(s.v, int) and s.v == 0:
                            rms(s)
                            pool.wait_ge(S["v_consts"], 32)
                        if s.exists():
                            pool.wait_ge(S["tanh_done"], s.v + 1)
                            settle(pool)
                            pool.tensor_scalar(sig[:], sig[:], 0.5, 0.5, ALU.mult, ALU.add).then_inc(S["sig_done"], 1)
                        if s.at(1).exists():
                            rms(s.at(1))
                        if s.at(-4).exists():
                            norm_consts(s.at(-4), ymv, yrs, "yagg", "ynormed", "yeps", "yrstd", "ynmr")
                        if s.exists():
                            norm_consts(s, vmv, vrs, "vagg", "vnormed", "veps", "vrstd", "vnmr")
                            pool.wait_ge(S["vnormed"], s.v + 1)
                            pool.tensor_tensor(vn[:], vn[:], gv[:], ALU.mult).then_inc(S["vgain"], 1)
                            pool.wait_ge(S["vgain"], s.v + 1)
                            pool.tensor_tensor(vn[:], vn[:], bv[:], ALU.add).then_inc(S["v_done"], 1)
                        t = s.at(-4)
                        if t.exists():
                            pool.wait_ge(x1_in[t.par], 16 * (t.half + 1))
                            for n in range(2):
                                pool.wait_ge(S["wo_read"], 2 * t.v + n + 1)
                                x = x1[t.par][:, 512 * n:512 * n + 512]
                                pool.tensor_tensor(x, mixed[:, 512 * n:512 * n + 512], x, ALU.add).then_inc(S["x1_half"], 1)
                    steps(pool, step, 6, 5, 21)

                @block.scalar
                def _(act):
                    def square(t):
                        act.wait_ge(S["x_here0"], 16 * (t.v + 1))
                        need(act, S["normed"], t.v)
                        act.activation(junk[:], x_in[0][:], ACT.Square, scale=1 / 32, accum_out=ss[:, t.par:t.par + 1]).then_inc(S["squares"], 1)

                    def norm(t):
                        act.wait_ge(S["rstd"], t.v + 1)
                        act.wait_ge(S["squares"], t.v + 1)
                        act.activation(xn[:], x_in[0][:], ACT.Copy, scale=rs[:, t.par:t.par + 1]).then_inc(S["normed"], 1)

                    def evac_hT(t, half):
                        act.wait_ge(S["turned"], 2 * t.v + half + 1)
                        if half == 0:
                            need(act, S["u_psum"], t.v - 1)
                        for j in range(4):
                            k = 4 * half + j
                            last = act.activation(hT[t.par][:, k, :], pst[:, j, :], ACT.Copy, scale=gcol[:, k:k + 1])
                        last.then_inc(S["hT_done"], 1)

                    def step(s):
                        if isinstance(s.v, int) and s.v == 0:
                            square(s)
                            norm(s)
                            evac_hT(s, 0)
                            evac_hT(s, 1)
                        if s.exists():
                            act.wait_ge(S["gate_psum"], s.v + 1)
                            need(act, S["a_done"], s.v)
                            act.activation(sig[:], psz[GATE][:], ACT.Tanh, scale=0.5).then_inc(S["tanh_done"], 1)
                        t = s.at(1)
                        if t.exists():
                            need(act, S["ynT_psum"], t.v - 5)
                            square(t)
                            norm(t)
                        t = s.at(-1)
                        if t.exists():
                            act.wait_ge(S["bT_psum"], t.v + 1)
                            need(act, S["mb_out"], 16 * t.v)
                            act.activation(mbT[:], psx[:], ACT.Copy).then_inc(S["mb_done"], 1)
                        t = s.at(-4)
                        if t.exists():
                            act.wait_ge(S["ynmr"], t.v + 1)
                            act.wait_ge(S["squares"], min_tile(s.v + 2))
                            act.activation(yn, psy[:].rearrange("p c n -> p (c n)"), ACT.Identity, bias=yrs[:, 1:2],
                                           scale=yrs[:, 0:1]).then_inc(S["ynormed"], 1)
                        if s.at(1).exists():
                            evac_hT(s.at(1), 0)
                        if s.exists():
                            act.wait_ge(S["vnmr"], s.v + 1)
                            need(act, S["sg_psum"], s.v)
                            act.activation(vn[:], psz[VV][:], ACT.Identity, bias=vrs[:, 1:2], scale=vrs[:, 0:1]).then_inc(S["vnormed"], 1)
                        if s.at(1).exists():
                            evac_hT(s.at(1), 1)
                        t = s.at(-4)
                        if t.exists():
                            act.wait_ge(S["ynT_psum"], t.v + 1)
                            need(act, S["wo_psum"], 2 * t.v)
                            for c in range(CG):
                                last = act.activation(maT[:, c, :], psx[:, c, :], ACT.Silu, bias=pcol[:, c, 33:34], scale=pcol[:, c, 32:33])
                            last.then_inc(S["ma_done"], 1)
                        if s.exists():
                            act.wait_ge(S["u_psum"], s.v + 1)
                            need(act, S["b_done"], s.v)
                            act.activation(u_sb[:], psz[UU][:], ACT.Copy).then_inc(S["u_done"], 1)
                            act.wait_ge(S["aT_psum"], s.v + 1)
                            if isinstance(s.v, int) and s.v == PT:
                                act.activation(sext[:, :, :, HIST:HIST + SLEN],
                                               psx[:].rearrange("p c (s r) -> p c s r", r=SLEN), ACT.Copy).then_inc(S["stage_full"], 1)
                            else:
                                need(act, S["ext_ready"], 2 * s.half)
                                act.activation(stage[s.par][:], psx[:], ACT.Copy).then_inc(S["stage_full"], 1)
                        t = s.at(-4)
                        if t.exists():
                            for n in range(2):
                                act.wait_ge(S["wo_psum"], 2 * t.v + n + 1)
                                need(act, S["x1_half"], 2 * t.v - 1 + n)
                                act.activation(mixed[:, 512 * n:512 * n + 512], psz[n][:], ACT.Copy).then_inc(S["wo_read"], 1)

                    def min_tile(v):
                        return v if not isinstance(v, int) else min(v, NT)
                    steps(act, step, 6, 5, 21)

                @block.vector
                def _(dve):
                    def conv(pair_half, first, taps):
                        base = pair_half * (4 * TAPS) + first * TAPS
                        for k in taps:
                            for i in range(2):
                                c = first + i
                                w = pcol[:, c, k:k + 1]
                                src = aext[:, c, k:k + 2 * P]
                                if k == 0:
                                    need(dve, S["conv_step"], base + i - 1)
                                    ins = dve.tensor_scalar(yacc[:, i, :], src, w, pcol[:, c, 31:32], ALU.mult, ALU.add)
                                else:
                                    dve.wait_ge(S["conv_step"], base + 2 * k - 1 + i)
                                    out = yacc[:, i, :]
                                    if k == TAPS - 1:
                                        if i == 0:
                                            need(dve, S["yT_psum"], 2 * pair_half)
                                        out = ybuf[:, c, :]
                                    ins = dve.scalar_tensor_tensor(out=out, in0=src, scalar=w, in1=yacc[:, i, :], op0=ALU.mult, op1=ALU.add)
                                ins.then_inc(S["conv_step"], 1)

                    def conv_sample():
                        base = (PT // 2) * 4 * TAPS
                        for k in range(TAPS):
                            for c in range(CG):
                                w = pcol[:, c, k:k + 1]
                                src = sext[:, c, :, k:k + SLEN]
                                acc = yacc[:, c // 2, P * (c % 2):P * (c % 2) + P].rearrange("p (s r) -> p s r", r=SLEN)
                                if k == 0:
                                    ins = dve.tensor_scalar(acc, src, w, pcol[:, c, 31:32], ALU.mult, ALU.add)
                                else:
                                    dve.wait_ge(S["conv_step"], base + 4 * (k - 1) + c + 1)
                                    out = acc
                                    if k == TAPS - 1:
                                        if c == 0:
                                            dve.wait_ge(S["yT_psum"], PT)
                                        out = ybuf[:, c, 0:P].rearrange("p (s r) -> p s r", r=SLEN)
                                    ins = dve.scalar_tensor_tensor(out=out, in0=src, scalar=w, in1=acc, op0=ALU.mult, op1=ALU.add)
                                ins.then_inc(S["conv_step"], 1)

                    dve.memset(aext[:, :, 0:HIST], 0.0).then_inc(S["halo"], 1)

                    def step(s):
                        static = isinstance(s.v, int)
                        t = s.at(-1)
                        if t.exists():
                            bias = bsg_s if isinstance(t.v, int) and t.v == PT else bsg
                            dve.wait_ge(S["sg_psum"], t.v + 1)
                            dve.wait_ge(S["u_done"], t.v + 1)
                            need(dve, S["bT_psum"], t.v)
                            for h in range(HEADS):
                                c = slice(P * h, P * h + P)
                                last = dve.scalar_tensor_tensor(out=b_tok[:, c], in0=psg[:, h, :], scalar=bias[:, h:h + 1],
                                                                in1=u_sb[:, c], op0=ALU.add, op1=ALU.mult)
                            last.then_inc(S["b_done"], 1)
                        if s.exists():
                            dve.wait_ge(S["val_psum"], s.v + 1)
                            dve.wait_ge(S["sig_done"], s.v + 1)
                            need(dve, S["aT_psum"], s.v - 1)
                            dve.tensor_tensor(a_tok[s.par][:], psz[VAL][:], sig[:], ALU.mult).then_inc(S["a_done"], 1)
                        t = s.at(-4)
                        if t.exists():
                            dve.wait_ge(S["yT_psum"], t.v + 1)
                            dve.bn_stats(yst[:], psy[:].rearrange("p c n -> p (c n)")).then_inc(S["ystat"], 1)
                            dve.wait_ge(S["ystat"], t.v + 1)
                            need(dve, S["ynmr"], t.v)
                            settle(dve)
                            dve.bn_aggr(ymv[:], yst[:]).then_inc(S["yagg"], 1)
                        q = s.at(-2)
                        if q.exists(PT) and s.par == 0:
                            if static and s.v == 2:
                                dve.wait_ge(S["halo"], 1)
                            else:
                                dve.wait_ge(S["conv_step"], q.half * 4 * TAPS)
                                dve.tensor_copy(aext[:, :, 0:HIST], aext[:, :, 2 * P:2 * P + HIST]).then_inc(S["halo"], 1)
                                dve.wait_ge(S["halo"], q.half + 1)
                            for i in range(2):
                                dve.wait_ge(S["stage_full"], q.v + i + 1)
                                dve.tensor_copy(aext[:, :, HIST + P * i:HIST + P * i + P], stage[i][:]).then_inc(S["ext_ready"], 1)
                            dve.wait_ge(S["ext_ready"], q.v + 2)
                        q = s.at(-2 - s.par)
                        if q.exists(PT):
                            conv(q.half, 2 * s.par, range(0, 8))
                        if static and s.v == PT + 2:
                            dve.wait_ge(S["stage_full"], NT)
                            dve.wait_ge(S["conv_step"], PT // 2 * 4 * TAPS)
                            conv_sample()
                        if s.exists():
                            dve.wait_ge(S["v_psum"], s.v + 1)
                            dve.bn_stats(vst[:], psz[VV][:]).then_inc(S["vstat"], 1)
                            dve.wait_ge(S["vstat"], s.v + 1)
                            need(dve, S["vnmr"], s.v)
                            settle(dve)
                            dve.bn_aggr(vmv[:], vst[:]).then_inc(S["vagg"], 1)
                        if q.exists(PT):
                            conv(q.half, 2 * s.par, range(8, TAPS))
                    steps(dve, step, 6, 5, 21)

                @block.tensor
                def _(pe):
                    def turn_x(t, half):
                        pe.wait_ge(S["normed"], t.v + 1)
                        need(pe, S["hT_done"], 2 * t.v + half)
                        for j in range(4):
                            k = 4 * half + j
                            last = pe.transpose(pst[:, j, :], xn[:, P * k:P * k + P], ident[:])
                        last.then_inc(S["turned"], 1)

                    def project(t, bank, done, free):
                        if isinstance(t.v, int) and t.v == 0:
                            pe.wait_ge(win_here, 64)
                        if bank == GATE:
                            pe.wait_ge(S["hT_done"], 2 * t.v + 2)
                        need(pe, S[free], t.v)
                        if bank in (GATE, VAL):
                            need(pe, S["wo_read"], 2 * (t.v - 5) + bank + 1)
                        for k in range(KD):
                            last = pe.matmul(psz[bank][:], hT[t.par][:, k, :], w_in[:, k, COL[bank]:COL[bank] + 512],
                                             start=(k == 0), stop=(k == KD - 1))
                        last.then_inc(S[done], 1)

                    def turn_y(t):
                        if isinstance(t.v, int) and t.v == PT:
                            pe.wait_ge(S["conv_step"], PT // 2 * 4 * TAPS + CG * TAPS)
                        else:
                            pe.wait_ge(S["conv_step"], (t.half + 1) * 4 * TAPS)
                        need(pe, S["ynormed"], t.v)
                        for c in range(CG):
                            last = pe.transpose(psy[:, c, :], ybuf[:, c, P * t.par:P * t.par + P], ident[:])
                        last.then_inc(S["yT_psum"], 1)

                    def step(s):
                        if isinstance(s.v, int) and s.v == 0:
                            turn_x(s, 0)
                            turn_x(s, 1)
                        if s.exists():
                            project(s, GATE, "gate_psum", "tanh_done")
                        t = s.at(-1)
                        if t.exists():
                            w = sgT_s if isinstance(t.v, int) and t.v == PT else sgT
                            pe.wait_ge(S["v_done"], t.v + 1)
                            need(pe, S["b_done"], t.v)
                            for h in range(HEADS):
                                last = pe.matmul(psg[:, h, :], w[:, h, :], vn[:, P * h:P * h + P], start=True, stop=True)
                            last.then_inc(S["sg_psum"], 1)
                        if s.exists():
                            project(s, VAL, "val_psum", "a_done")
                        t = s.at(-4)
                        if t.exists():
                            turn_y(t)
                        t = s.at(-1)
                        if t.exists():
                            pe.wait_ge(S["b_done"], t.v + 1)
                            pe.wait_ge(S["stage_full"], t.v + 1)
                            for c in range(CG):
                                last = pe.transpose(psx[:, c, :], b_tok[:, P * c:P * c + P], ident[:])
                            last.then_inc(S["bT_psum"], 1)
                        if s.at(1).exists():
                            turn_x(s.at(1), 0)
                        if s.exists():
                            project(s, VV, "v_psum", "vnormed")
                        if s.at(1).exists():
                            turn_x(s.at(1), 1)
                        t = s.at(-4)
                        if t.exists():
                            pe.wait_ge(S["ynormed"], t.v + 1)
                            if s.at(-1).exists():
                                pe.wait_ge(S["mb_done"], s.v)
                            else:
                                pe.wait_ge(S["mb_done"], NT)
                                need(pe, S["ma_done"], t.v)
                            for c in range(CG):
                                last = pe.transpose(psx[:, c, :], yn[:, P * c:P * c + P], ident[:])
                            last.then_inc(S["ynT_psum"], 1)
                        if s.exists():
                            project(s, UU, "u_psum", "u_done")
                            pe.wait_ge(S["a_done"], s.v + 1)
                            need(pe, S["ma_done"], s.v - 3)
                            need(pe, S["mb_done"], s.v)
                            for c in range(CG):
                                last = pe.transpose(psx[:, c, :], a_tok[s.par][:, P * c:P * c + P], ident[:])
                            last.then_inc(S["aT_psum"], 1)
                        t = s.at(-4)
                        if t.exists():
                            if isinstance(t.v, int) and t.v == 0:
                                pe.wait_ge(wout_here, 16)
                            pe.wait_ge(S["ma_done"], t.v + 1)
                            pe.wait_ge(mbl_here[t.par], 16 * (t.half + 1))
                            if s.exists():
                                pe.wait_ge(S["tanh_done"], s.v + 1)
                            for n in range(2):
                                need(pe, S["wo_read"], 2 * t.v - 1 + n)
                                for k in range(KD):
                                    last = pe.matmul(psz[n][:], (maT[:, k, :] if k < CG else mbl[t.par][:, k - CG, :]),
                                                     w_out[:, k, 512 * n:512 * n + 512], start=(k == 0), stop=(k == KD - 1))
                                last.then_inc(S["wo_psum"], 1)
                    steps(pe, step, 6, 5, 21)
        mix_stack.close()

        only_seq = W[:, 16384:24576].rearrange("p (s c n) -> p s c n", s=SEQS, c=8)
        q_stack = ExitStack()
        sbq, _, _ = alloc(q_stack)
        qT = sbq("qT", [P, 8, P])
        with one_stage() as st:
            sb, pb, sem = alloc(st)
            x1 = [sb(f"b_x1{i}", [P, D]) for i in range(2)]
            xn = spare[0]
            h2T = spare[1].rearrange("p (k n) -> p k n", k=KD)
            prob = spare[2].rearrange("p (h n) -> p h n", h=HEADS)
            pT = spare[3].rearrange("p (c n) -> p c n", c=8)
            oT = sb("b_oT", [P, 8, P])
            ss = sb("b_ss", [P, 1])
            rs = sb("b_rs", [P, 2])
            mx = sb("b_mx", [P, HEADS])
            nb = sb("b_nb", [P, HEADS])
            sm = sb("b_sm", [P, HEADS])
            rc = sb("b_rc", [P, HEADS])
            pso = pb("b_pso", [P, D])
            pss = pb("b_pss", [P, HEADS, NMEM])
            psq = pb("b_psq", [P, 8, P])
            pst = pb("b_pst", [P, 8, P])
            names = ("squares eps rstd normed turned h2T_done q_psum qT_done "
                     "s_psum max_done nb_done exp_done rc_done prob_done pT_psum pT_done o_psum oT_done oT_out").split()
            S = {n: sem("b_" + n) for n in names}
            x1_here = [sem(f"b_x1_here{i}") for i in range(2)]
            with nc.Block() as block:
                @block.sync
                def _(sp):
                    def load(t):
                        need(sp, S["normed"], t.v - 1)
                        settle(sp)
                        sp.dma_start(x1[t.par][:], row(x1_d, t)).then_inc(x1_here[t.par], 16)

                    def step(s):
                        if isinstance(s.v, int) and s.v == 0:
                            load(s)
                            load(s.at(1))
                        if s.at(2).exists():
                            load(s.at(2))
                        t = s.at(-2)
                        if t.exists(PT):
                            sp.wait_ge(S["oT_done"], t.v + 1)
                            sp.dma_start(row(oT_d, t), oT[:].rearrange("p c n -> p (c n)")).then_inc(S["oT_out"], 16)
                    steps(sp, step, 4, 5, NT + 1)
                    sp.wait_ge(S["oT_out"], 16 * PT)
                    sp.wait_ge(wr_here, 16 * (NG + 3))

                @block.gpsimd
                def _(pool):
                    pool.memset(W[:, 16384:24576], 0.0).then_inc(only_zero, 1)

                    def step(t):
                        pool.wait_ge(S["squares"], t.v + 1)
                        need(pool, S["normed"], t.v)
                        settle(pool)
                        pool.tensor_scalar(rs[:, 0:1], ss[:], EPS, None, ALU.add).then_inc(S["eps"], 1)
                        pool.wait_ge(S["eps"], t.v + 1)
                        pool.tensor_tensor(rs[:, 1:2], rs[:, 0:1], mhalf[:], ALU.pow).then_inc(S["rstd"], 1)
                    steps(pool, step, 4, 6, NT)

                @block.scalar
                def _(act):
                    act.dma_start(br[:, 0:NG], I["b_router_group"].partition_broadcast(P).rearrange("p a d -> p (a d)")).then_inc(wr_here, 16)
                    act.dma_start(br[:, NG:NG + NE], I["b_router_expert"].partition_broadcast(P).rearrange("p a g e -> p (a g e)")).then_inc(wr_here, 16)
                    act.dma_start(wr[:, :, 0:NG], I["w_router_group"][0].rearrange("(k p) g -> p k g", p=P)).then_inc(wr_here, 16)
                    for g in range(NG):
                        act.dma_start(wr[:, :, NG + EPG * g:NG + EPG * g + EPG], I["w_router_expert"][0, g].rearrange("(k p) e -> p k e", p=P)).then_inc(wr_here, 16)

                    def norm(t):
                        act.wait_ge(x1_here[t.par], 16 * (t.half + 1))
                        need(act, S["turned"], t.v)
                        act.activation(xn[:], x1[t.par][:], ACT.Square, scale=1 / 32, accum_out=ss[:]).then_inc(S["squares"], 1)
                        act.wait_ge(S["rstd"], t.v + 1)
                        act.wait_ge(S["squares"], t.v + 1)
                        act.activation(xn[:], x1[t.par][:], ACT.Copy, scale=rs[:, 1:2]).then_inc(S["normed"], 1)

                    def step(s):
                        if isinstance(s.v, int) and s.v == 0:
                            norm(s)
                        t = s.at(-2)
                        if t.exists(PT):
                            act.wait_ge(S["pT_psum"], t.v + 1)
                            need(act, S["o_psum"], t.v)
                            act.activation(pT[:], psq[:], ACT.Copy).then_inc(S["pT_done"], 1)
                        t = s.at(-1)
                        if t.exists(PT):
                            act.wait_ge(S["nb_done"], t.v + 1)
                            need(act, S["pT_psum"], t.v)
                            need(act, S["prob_done"], t.v)
                            for h in range(HEADS):
                                last = act.activation(prob[:, h, :], pss[:, h, :], ACT.Exp, bias=nb[:, h:h + 1], scale=SCALE,
                                                      accum_out=sm[:, h:h + 1])
                            last.then_inc(S["exp_done"], 1)
                        t = s.at(-2)
                        if t.exists(PT):
                            act.wait_ge(S["o_psum"], t.v + 1)
                            need(act, S["oT_out"], 16 * t.v)
                            act.activation(oT[:], pso[:].rearrange("p (c n) -> p c n", c=8), ACT.Copy).then_inc(S["oT_done"], 1)
                        if s.at(1).exists():
                            norm(s.at(1))
                        if s.exists():
                            act.wait_ge(S["q_psum"], s.v + 1)
                            need(act, S["s_psum"], s.v)
                            act.activation(qT[:], psq[:], ACT.Copy).then_inc(S["qT_done"], 1)
                    steps(act, step, 4, 6, NT + 1)

                @block.vector
                def _(dve):
                    def step(s):
                        if s.exists():
                            dve.wait_ge(S["turned"], s.v + 1)
                            need(dve, S["q_psum"], s.v)
                            dve.tensor_tensor(h2T[:], pst[:], gcol[:, 8:16].unsqueeze(2).to_broadcast([P, KD, P]), ALU.mult).then_inc(S["h2T_done"], 1)
                        t = s.at(-1)
                        if t.exists(PT):
                            dve.wait_ge(S["s_psum"], t.v + 1)
                            need(dve, S["nb_done"], t.v)
                            dve.tensor_reduce(mx[:], pss[:], X, ALU.max).then_inc(S["max_done"], 1)
                            dve.wait_ge(S["max_done"], t.v + 1)
                            need(dve, S["exp_done"], t.v)
                            dve.tensor_scalar(nb[:], mx[:], -SCALE, None, ALU.mult).then_inc(S["nb_done"], 1)
                            dve.wait_ge(S["exp_done"], t.v + 1)
                            need(dve, S["prob_done"], t.v)
                            dve.reciprocal(rc[:], sm[:]).then_inc(S["rc_done"], 1)
                            dve.wait_ge(S["rc_done"], t.v + 1)
                            dve.tensor_tensor(prob[:], prob[:], rc[:].unsqueeze(2).to_broadcast([P, HEADS, NMEM]), ALU.mult).then_inc(S["prob_done"], 1)
                    steps(dve, step, 4, 6, NT + 1)

                @block.tensor
                def _(pe):
                    pe.wait_ge(wxq_here, 16)

                    def step(s):
                        if s.exists():
                            pe.wait_ge(S["normed"], s.v + 1)
                            need(pe, S["h2T_done"], s.v)
                            for k in range(KD):
                                last = pe.transpose(pst[:, k, :], xn[:, P * k:P * k + P], ident[:])
                            last.then_inc(S["turned"], 1)
                        t = s.at(-2)
                        if t.exists(PT):
                            pe.wait_ge(S["prob_done"], t.v + 1)
                            pe.wait_ge(S["qT_done"], t.v + 2)
                            for h in range(HEADS):
                                for m in range(2):
                                    last = pe.transpose(psq[:, 2 * h + m, :], prob[:, h, P * m:P * m + P], ident[:])
                            last.then_inc(S["pT_psum"], 1)
                        t = s.at(-1)
                        if t.exists(PT):
                            pe.wait_ge(S["qT_done"], t.v + 1)
                            need(pe, S["exp_done"], t.v)
                            for h in range(HEADS):
                                for k in range(2):
                                    last = pe.matmul(pss[:, h, :], qT[:, 2 * h + k, :], KT[:, 2 * h + k, :], start=(k == 0), stop=(k == 1))
                            last.then_inc(S["s_psum"], 1)
                        t = s.at(-2)
                        if t.exists(PT):
                            pe.wait_ge(S["pT_done"], t.v + 1)
                            need(pe, S["oT_done"], t.v)
                            for c in range(8):
                                for m in range(2):
                                    last = pe.matmul(pso[:, P * c:P * c + P], V[:, m, P * c:P * c + P], pT[:, c // 2 * 2 + m, :],
                                                     start=(m == 0), stop=(m == 1))
                            last.then_inc(S["o_psum"], 1)
                        if s.exists():
                            pe.wait_ge(S["h2T_done"], s.v + 1)
                            need(pe, S["qT_done"], s.v)
                            for c in range(8):
                                for k in range(KD):
                                    last = pe.matmul(psq[:, c, :], w_xq[:, k, P * c:P * c + P], h2T[:, k, :],
                                                     start=(k == 0), stop=(k == KD - 1))
                            last.then_inc(S["q_psum"], 1)
                    steps(pe, step, 4, 6, NT + 1)
        with one_stage() as st:
            sb, pb, sem = alloc(st)
            kv = [W[:, c:c + 2 * D].rearrange("p (m d) -> p m d", m=2)
                  for c in [24576 + 2 * D * i for i in range(6)] + [8192, 8192 + 2 * D]]
            KTs = [sb(f"s_KT{i}", [P, 8, NMEM]) for i in range(2)]
            only = only_seq
            prob = sb("s_prob", [P, HEADS, NMEM])
            o_tok = sb("s_otok", [P, D])
            oT = sb("s_oT", [P, 8, P])
            mx = sb("s_mx", [P, HEADS])
            nb = sb("s_nb", [P, HEADS])
            sm = sb("s_sm", [P, HEADS])
            rc = sb("s_rc", [P, HEADS])
            psa = pb("s_psa", [P, 8, P])
            psb = pb("s_psb", [P, 8, P])
            pss = pb("s_pss", [P, HEADS, NMEM])
            pso = pb("s_pso", [P, D])
            kv_here = [sem(f"s_kv_here{i}") for i in range(SEQS)]
            S = {n: sem("s_" + n) for n in ("q_only ka_psum kb_psum ka_done kb_done s_psum o_psum o_done oT_psum max_done nb_done "
                                            "exp_done rc_done prob_done pT_psum pT_done oT_done oT_out").split()}
            with nc.Block() as block:
                @block.sync
                def _(sp):
                    def load(cache, s):
                        sp.dma_start(kv[s], I[cache][0][s].rearrange("(m p) h d -> p m (h d)", p=P)).then_inc(kv_here[s], 16)
                    for s in range(SEQS):
                        load("cache_mem_k", s)
                    for s in range(SEQS):
                        sp.wait_ge(S["kb_psum"], s + 1)
                        load("cache_mem_v", s)
                    sp.wait_ge(S["oT_done"], 1)
                    sp.dma_start(oT_d[PT, :, :], oT[:].rearrange("p c n -> p (c n)")).then_inc(S["oT_out"], 16)
                    sp.wait_ge(S["oT_out"], 16)

                def spread(copy, src, half, name):
                    for q in range(SEQS):
                        cols = slice(SLEN * q, SLEN * q + SLEN)
                        chunks = slice(4 * half, 4 * half + 4)
                        copy(only[:, q, chunks, cols], src[:, chunks, cols]).then_inc(S[name], 1)

                @block.scalar
                def _(act):
                    def copy(out, src):
                        return act.activation(out, src, ACT.Copy)

                    def step(s):
                        act.wait_ge(S["ka_psum"], s.v + 1)
                        need(act, S["s_psum"], s.v - 1)
                        act.activation(KTs[s.par][:, :, 0:P], psa[:], ACT.Copy).then_inc(S["ka_done"], 1)
                    act.wait_ge(only_zero, 1)
                    spread(copy, qT, 0, "q_only")
                    steps(act, step, 2, 3, SEQS)
                    act.wait_ge(S["nb_done"], 1)
                    for h in range(HEADS):
                        last = act.activation(prob[:, h, :], pss[:, h, :], ACT.Exp, bias=nb[:, h:h + 1], scale=SCALE,
                                              accum_out=sm[:, h:h + 1])
                    last.then_inc(S["exp_done"], 1)
                    act.wait_ge(S["pT_psum"], 1)
                    spread(copy, psa, 0, "pT_done")
                    act.wait_ge(S["o_psum"], 1)
                    act.activation(o_tok[:, 0:512], pso[:, 0:512], ACT.Copy).then_inc(S["o_done"], 1)
                    act.wait_ge(S["oT_psum"], 1)
                    act.activation(oT[:], psb[:], ACT.Copy).then_inc(S["oT_done"], 1)

                @block.vector
                def _(dve):
                    def step(s):
                        dve.wait_ge(S["kb_psum"], s.v + 1)
                        need(dve, S["s_psum"], s.v - 1)
                        dve.tensor_copy(KTs[s.par][:, :, P:2 * P], psb[:]).then_inc(S["kb_done"], 1)
                    dve.wait_ge(only_zero, 1)
                    spread(dve.tensor_copy, qT, 1, "q_only")
                    steps(dve, step, 2, 3, SEQS)
                    dve.wait_ge(S["s_psum"], SEQS)
                    dve.tensor_reduce(mx[:], pss[:], X, ALU.max).then_inc(S["max_done"], 1)
                    dve.wait_ge(S["max_done"], 1)
                    dve.tensor_scalar(nb[:], mx[:], -SCALE, None, ALU.mult).then_inc(S["nb_done"], 1)
                    dve.wait_ge(S["exp_done"], 1)
                    dve.reciprocal(rc[:], sm[:]).then_inc(S["rc_done"], 1)
                    dve.wait_ge(S["rc_done"], 1)
                    dve.tensor_tensor(prob[:], prob[:], rc[:].unsqueeze(2).to_broadcast([P, HEADS, NMEM]), ALU.mult).then_inc(S["prob_done"], 1)
                    dve.wait_ge(S["pT_psum"], 1)
                    spread(dve.tensor_copy, psa, 1, "pT_done")
                    dve.wait_ge(S["o_psum"], 1)
                    dve.tensor_copy(o_tok[:, 512:1024], pso[:, 512:1024]).then_inc(S["o_done"], 1)

                @block.tensor
                def _(pe):
                    def turn_keys(s):
                        pe.wait_ge(kv_here[s.v], 16)
                        need(pe, S["ka_done"], s.v)
                        for k in range(8):
                            last = pe.transpose(psa[:, k, :], kv[s.v][:, 0, P * k:P * k + P], ident[:])
                        last.then_inc(S["ka_psum"], 1)
                        need(pe, S["kb_done"], s.v)
                        for k in range(8):
                            last = pe.transpose(psb[:, k, :], kv[s.v][:, 1, P * k:P * k + P], ident[:])
                        last.then_inc(S["kb_psum"], 1)

                    def scores(s):
                        pe.wait_ge(S["ka_done"], s.v + 1)
                        pe.wait_ge(S["kb_done"], s.v + 1)
                        for h in range(HEADS):
                            for k in range(2):
                                last = pe.matmul(pss[:, h, :], only[:, s.v, 2 * h + k, :], KTs[s.par][:, 2 * h + k, :],
                                                 start=(s.v == 0 and h % 2 == 0 and k == 0), stop=(s.v == SEQS - 1 and h % 2 == 1 and k == 1))
                        last.then_inc(S["s_psum"], 1)

                    turn_keys(fixed(0))
                    pe.wait_ge(S["q_only"], 2 * SEQS)
                    for q in range(SEQS):
                        if q + 1 < SEQS:
                            turn_keys(fixed(q + 1))
                        scores(fixed(q))
                    pe.wait_ge(S["prob_done"], 1)
                    pe.wait_ge(S["ka_done"], SEQS)
                    for h in range(HEADS):
                        for m in range(2):
                            last = pe.transpose(psa[:, 2 * h + m, :], prob[:, h, P * m:P * m + P], ident[:])
                    last.then_inc(S["pT_psum"], 1)
                    pe.wait_ge(S["pT_done"], 2 * SEQS)
                    for q in range(SEQS):
                        pe.wait_ge(kv_here[q], 32)
                        for h in range(HEADS):
                            for m in range(2):
                                last = pe.matmul(pso[:, HD * h:HD * h + HD], only[:, q, 2 * h + m, :], kv[q][:, m, HD * h:HD * h + HD],
                                                 start=(q == 0 and h % 2 == 0 and m == 0), stop=(q == SEQS - 1 and h % 2 == 1 and m == 1))
                    last.then_inc(S["o_psum"], 1)
                    pe.wait_ge(S["o_done"], 2)
                    for c in range(8):
                        last = pe.transpose(psb[:, c, :], o_tok[:, P * c:P * c + P], ident[:])
                    last.then_inc(S["oT_psum"], 1)
        q_stack.close()
        kv_stack.close()
        e_stack = ExitStack()
        sbe, _, seme = alloc(e_stack)
        gu_d = (I["w_expert_gate"][0], I["w_expert_up"][0])
        expert_here = [seme(f"expert_here{i}") for i in range(2)]

        def load_expert(eng, e, slot, par):
            base = W[:, EXPERT_COLS * slot:EXPERT_COLS * slot + EXPERT_COLS]
            for n, name in enumerate(("w_expert_gate", "w_expert_up")):
                eng.dma_start(base[:, 4096 * n:4096 * n + 4096].rearrange("p (k n) -> p k n", k=KD),
                              I[name][0][bass.ds(e, 1), :, :].rearrange("a (k p) n -> p (a k) n", p=P)).then_inc(expert_here[par], 16)
            eng.dma_start(base[:, 8192:12288].rearrange("p (k n) -> p k n", k=KE),
                          I["w_expert_down"][0][bass.ds(e, 1), :, :].rearrange("a (k p) n -> p (a k) n", p=P)).then_inc(expert_here[par], 16)

        with one_stage() as st:
            sb, pb, sem = alloc(st)
            oT = [sb(f"r_oT{i}", [P, 8, P]) for i in range(2)]
            x1 = [sb(f"r_x1{i}", [P, D]) for i in range(2)]
            x2 = [sb(f"r_x2{i}", [P, D]) for i in range(2)]
            h3 = [sb(f"r_h3{i}", [P, D]) for i in range(2)]
            junk = sb("r_junk", [P, D])
            h3T = sb("r_h3T", [P, KD, P])
            gf = sb("r_gffn", [P, D])
            ss = sb("r_ss", [P, 2])
            rs = sb("r_rs", [P, 2])
            lower = sb("r_lower", [P, P])
            iota4 = sb("r_iota4", [P, NG])
            iota32 = sb("r_iota32", [P, NE])
            pairs_i = sb("r_pairs", [P, NT, 2], I32)
            lg8 = sb("r_lg8", [P, 8])
            le = sb("r_le", [P, NE])
            gm8 = sb("r_gm8", [P, 8])
            gi8 = sb("r_gi8", [P, 8], U32)
            gif = sb("r_gif", [P, 2])
            ngm = sb("r_ngm", [P, 1])
            eg = sb("r_eg", [P, NG])
            gsum = sb("r_gsum", [P, 1])
            goh = sb("r_goh", [P, NG])
            lsel = sb("r_lsel", [P, EPG, NG])
            le8 = sb("r_le8", [P, EPG])
            v8 = sb("r_v8", [P, 8])
            i8 = sb("r_i8", [P, 8], U32)
            i2f = sb("r_i2f", [P, 2])
            nv1 = sb("r_nv1", [P, 1])
            e2 = sb("r_e2", [P, 1])
            den = sb("r_den", [P, 2])
            ef = [sb(f"r_ef{i}", [P, 2]) for i in range(2)]
            oh = [sb(f"r_oh{i}", [P, 2, NE]) for i in range(2)]
            picked = [sb(f"r_picked{i}", [P, NE]) for i in range(2)]
            rk = sb("r_rk", [P, 2, NE])
            rank = sb("r_rank", [P, 2])
            slotf = sb("r_slotf", [P, 2])
            slot_i = [sb(f"r_slot{i}", [P, 2], I32) for i in range(2)]
            val = [sb(f"r_val{i}", [P, 2], I32) for i in range(2)]
            psx = [pb(f"r_psx{i}", [P, D]) for i in range(2)]
            pst = pb("r_pst", [P, KD, P])
            psr = pb("r_psr", [P, 512])
            psk = pb("r_psk", [P, 512])
            names = ("consts iotas o_psum x2_done squares eps rstd h3_done turned h3T_done r_psum lg_done gmax gidx gif gexp "
                     "goh lsel le8 v8 i8 i2f ef oh picked gexp2 den gate1 gate2 rank_psum rk rank slotf slot total_done ngm "
                     "nv1 pads rank2").split()
            S = {n: sem("r_" + n) for n in names}
            oT_here = [sem(f"r_oT_here{i}") for i in range(2)]
            x1_here = [sem(f"r_x1_here{i}") for i in range(2)]
            x2_out = [sem(f"r_x2_out{i}") for i in range(2)]
            h3_out = [sem(f"r_h3_out{i}") for i in range(2)]
            scattered = [sem(f"r_scattered{i}") for i in range(2)]
            with nc.Block() as block:
                @block.sync
                def _(sp):
                    def load(t):
                        need(sp, S["o_psum"], t.v - 1)
                        sp.dma_start(oT[t.par][:].rearrange("p c n -> p (c n)"), row(oT_d, t)).then_inc(oT_here[t.par], 16)
                        need(sp, S["x2_done"], t.v - 1)
                        sp.dma_start(x1[t.par][:], row(x1_d, t)).then_inc(x1_here[t.par], 16)

                    def step(s):
                        if isinstance(s.v, int) and s.v == 0:
                            load(s)
                            load(s.at(1))
                        elif s.at(1).exists():
                            load(s.at(1))
                        if isinstance(s.v, int) and s.v in (1, 16):
                            load_expert(sp, s.v // 16, 1 + s.v // 16, s.v // 16)
                        sp.wait_ge(S["x2_done"], s.v + 1)
                        sp.dma_start(row(x2_d, s), x2[s.par][:]).then_inc(x2_out[s.par], 16)
                        sp.wait_ge(S["h3_done"], s.v + 1)
                        sp.dma_start(h3_d[bass.ds(P * s.v, P), :], h3[s.par][:]).then_inc(h3_out[s.par], 16)
                    steps(sp, step, 4, 6, NT)
                    for i in range(2):
                        sp.wait_ge(x2_out[i], 16 * (9 - i))
                        sp.wait_ge(h3_out[i], 16 * (9 - i))

                @block.gpsimd
                def _(pool):
                    pool.iota(iota4[:], [[1, NG]], base=0, channel_multiplier=0, allow_small_or_imprecise_dtypes=True).then_inc(S["iotas"], 1)
                    pool.iota(iota32[:], [[1, NE]], base=0, channel_multiplier=0, allow_small_or_imprecise_dtypes=True).then_inc(S["iotas"], 1)
                    pool.affine_select(out=lower[:], in_=ones[:], compare_op=ALU.is_gt, fill=0.0, base=0,
                                       pattern=[[1, P]], channel_multiplier=-1).then_inc(S["iotas"], 1)
                    pool.iota(pairs_i[:], [[2 * P, NT], [1, 2]], base=0, channel_multiplier=2).then_inc(S["iotas"], 1)

                    def step(s):
                        if s.exists():
                            pool.wait_ge(S["squares"], s.v + 1)
                            need(pool, S["h3_done"], s.v)
                            settle(pool)
                            pool.tensor_scalar(rs[:, 0:1], ss[:, 0:1], EPS, None, ALU.add).then_inc(S["eps"], 1)
                            pool.wait_ge(S["eps"], s.v + 1)
                            pool.tensor_tensor(rs[:, 1:2], rs[:, 0:1], mhalf[:], ALU.pow).then_inc(S["rstd"], 1)
                        t = s.at(-2)
                        if t.exists():
                            pool.wait_ge(S["slot"], t.v + 1)
                            for k in range(2):
                                settle(pool)
                                pool.indirect_dma_start(out=table_d, out_offset=bass.IndirectOffsetOnAxis(ap=slot_i[t.par][:, k:k + 1], axis=0),
                                                        in_=val[t.par][:, k:k + 1], in_offset=None).then_inc(scattered[t.par], 16)
                    steps(pool, step, 4, 6, NT + 2)
                    for i in range(2):
                        pool.wait_ge(scattered[i], 32 * (9 - i))

                @block.scalar
                def _(act):
                    act.dma_start(gf[:], I["g_ffn"].partition_broadcast(P).rearrange("p a d -> p (a d)")).then_inc(S["consts"], 16)

                    def step(s):
                        t = s.at(-1)
                        if t.exists():
                            act.wait_ge(S["turned"], t.v + 1)
                            need(act, S["r_psum"], t.v)
                            act.activation(h3T[:], pst[:], ACT.Copy).then_inc(S["h3T_done"], 1)
                        if s.exists():
                            act.wait_ge(S["x2_done"], s.v + 1)
                            need(act, S["rstd"], s.v)
                            need(act, S["squares"], s.v)
                            act.activation(junk[:], x2[s.par][:], ACT.Square, scale=1 / 32, accum_out=ss[:, 0:1]).then_inc(S["squares"], 1)
                        if t.exists():
                            act.wait_ge(S["ngm"], t.v + 1)
                            need(act, S["gate2"], t.v)
                            act.activation(eg[:], lg8[:, 0:NG], ACT.Exp, bias=ngm[:], accum_out=gsum[:]).then_inc(S["gexp"], 1)
                            act.wait_ge(S["nv1"], t.v + 1)
                            act.activation(e2[:], v8[:, 1:2], ACT.Exp, bias=nv1[:]).then_inc(S["gexp2"], 1)
                    steps(act, step, 4, 6, NT + 1)

                @block.vector
                def _(dve):
                    dve.memset(lg8[:], LOW).then_inc(S["pads"], 1)
                    dve.wait_ge(S["pads"], 1)
                    dve.wait_ge(S["consts"], 16)
                    dve.wait_ge(wr_here, 16 * (NG + 3))
                    dve.wait_ge(S["iotas"], 4)

                    def put(ins, name):
                        ins.then_inc(S[name], 1)

                    def route(t):
                        n = t.v + 1
                        dve.wait_ge(S["r_psum"], n)
                        need(dve, S["gexp"], t.v)
                        put(dve.tensor_tensor(lg8[:, 0:NG], psr[:, 0:NG], br[:, 0:NG], ALU.add), "lg_done")
                        put(dve.tensor_tensor(le[:], psr[:, NG:NG + NE], br[:, NG:NG + NE], ALU.add), "lg_done")
                        dve.wait_ge(S["lg_done"], 2 * t.v + 2)
                        settle(dve)
                        put(dve.max(gm8[:], lg8[:]), "gmax")
                        dve.wait_ge(S["gmax"], n)
                        put(dve.tensor_scalar(ngm[:], gm8[:, 0:1], -1.0, None, ALU.mult), "ngm")
                        put(dve.max_index(gi8[:], gm8[:], lg8[:]), "gidx")
                        dve.wait_ge(S["gidx"], n)
                        put(dve.tensor_copy(gif[:, 0:1], gi8[:, 0:1]), "gif")
                        dve.wait_ge(S["gif"], 2 * t.v + 1)
                        put(dve.tensor_scalar(goh[:], iota4[:], gif[:, 0:1], None, ALU.is_equal), "goh")
                        put(dve.tensor_scalar(gif[:, 1:2], gif[:, 0:1], float(EPG), None, ALU.mult), "gif")
                        dve.wait_ge(S["goh"], n)
                        put(dve.tensor_tensor(lsel[:], le[:].rearrange("p (g e) -> p e g", g=NG),
                                              goh[:].unsqueeze(1).to_broadcast([P, EPG, NG]), ALU.mult), "lsel")
                        dve.wait_ge(S["lsel"], n)
                        put(dve.tensor_reduce(le8[:], lsel[:], X, ALU.add), "le8")
                        dve.wait_ge(S["le8"], n)
                        need(dve, S["gexp2"], t.v)
                        settle(dve)
                        put(dve.max(v8[:], le8[:]), "v8")
                        dve.wait_ge(S["v8"], n)
                        put(dve.tensor_scalar(nv1[:], v8[:, 0:1], -1.0, None, ALU.mult), "nv1")
                        put(dve.max_index(i8[:], v8[:], le8[:]), "i8")
                        dve.wait_ge(S["i8"], n)
                        put(dve.tensor_copy(i2f[:], i8[:, 0:2]), "i2f")
                        dve.wait_ge(S["i2f"], n)
                        dve.wait_ge(S["gif"], 2 * t.v + 2)
                        put(dve.tensor_scalar(ef[t.par][:], i2f[:], gif[:, 1:2], None, ALU.add), "ef")
                        dve.wait_ge(S["ef"], n)
                        put(dve.tensor_tensor(oh[t.par][:], iota32[:].unsqueeze(1).to_broadcast([P, 2, NE]),
                                              ef[t.par][:].unsqueeze(2).to_broadcast([P, 2, NE]), ALU.is_equal), "oh")
                        dve.wait_ge(S["oh"], n)
                        put(dve.tensor_tensor(picked[t.par][:], oh[t.par][:, 0, :], oh[t.par][:, 1, :], ALU.add), "picked")
                        dve.wait_ge(S["gexp"], n)
                        dve.wait_ge(S["gexp2"], n)
                        put(dve.tensor_scalar(den[:, 0:1], e2[:], 1.0, gsum[:], ALU.add, ALU.mult), "den")
                        dve.wait_ge(S["den"], n)
                        g = gates[:, bass.ds(t.v, 1), :].rearrange("p a k -> p (a k)")
                        put(dve.reciprocal(g[:, 0:1], den[:, 0:1]), "gate1")
                        dve.wait_ge(S["gate1"], n)
                        put(dve.tensor_tensor(g[:, 1:2], g[:, 0:1], e2[:], ALU.mult), "gate2")

                    def place(t):
                        n = t.v + 1
                        dve.wait_ge(S["rank_psum"], n)
                        dve.wait_ge(S["oh"], n)
                        put(dve.tensor_tensor(rk[:], oh[t.par][:], psk[:, 0:NE].unsqueeze(1).to_broadcast([P, 2, NE]), ALU.mult), "rk")
                        put(dve.tensor_tensor(total[:], total[:], picked[t.par][:], ALU.add), "total_done")
                        dve.wait_ge(S["rk"], n)
                        put(dve.tensor_reduce(rank[:], rk[:], X, ALU.add), "rank")
                        dve.wait_ge(S["rank"], n)
                        put(dve.scalar_tensor_tensor(out=slotf[:], in0=ef[t.par][:], scalar=float(CAP), in1=rank[:], op0=ALU.mult, op1=ALU.add), "slotf")
                        need(dve, scattered[t.par], 32 * t.half)
                        put(dve.tensor_copy(val[t.par][:], pairs_i[:, bass.ds(t.v, 1), :].rearrange("p a k -> p (a k)")), "rank2")
                        dve.wait_ge(S["slotf"], n)
                        dve.wait_ge(S["rank2"], n)
                        put(dve.tensor_copy(slot_i[t.par][:], slotf[:]), "slot")

                    def step(s):
                        if s.exists():
                            dve.wait_ge(S["o_psum"], s.v + 1)
                            dve.wait_ge(x1_here[s.par], 16 * (s.half + 1))
                            need(dve, x2_out[s.par], 16 * s.half)
                            dve.tensor_tensor(x2[s.par][:], psx[s.par][:], x1[s.par][:], ALU.add).then_inc(S["x2_done"], 1)
                        t = s.at(-2)
                        if t.exists():
                            place(t)
                        if s.exists():
                            dve.wait_ge(S["rstd"], s.v + 1)
                            need(dve, h3_out[s.par], 16 * s.half)
                            need(dve, S["turned"], s.v - 1)
                            dve.scalar_tensor_tensor(out=h3[s.par][:], in0=x2[s.par][:], scalar=rs[:, 1:2], in1=gf[:],
                                                     op0=ALU.mult, op1=ALU.mult).then_inc(S["h3_done"], 1)
                        t = s.at(-1)
                        if t.exists():
                            route(t)
                    steps(dve, step, 4, 6, NT + 2)

                @block.tensor
                def _(pe):
                    pe.wait_ge(wxo_here, 16)
                    pe.wait_ge(wr_here, 16 * (NG + 3))

                    def half_xo(s, n):
                        for k in range(KD):
                            last = pe.matmul(psx[s.par][:, 512 * n:512 * n + 512], oT[s.par][:, k, :],
                                             w_xo[:, k, 512 * n:512 * n + 512], start=(k == 0), stop=(k == KD - 1))
                        return last

                    def step(s):
                        if s.exists():
                            pe.wait_ge(oT_here[s.par], 16 * (s.half + 1))
                            need(pe, S["x2_done"], s.v - 1)
                            half_xo(s, 0)
                        t = s.at(-1)
                        if t.exists():
                            pe.wait_ge(S["h3_done"], t.v + 1)
                            need(pe, S["h3T_done"], t.v)
                            for k in range(KD):
                                last = pe.transpose(pst[:, k, :], h3[t.par][:, P * k:P * k + P], ident[:])
                            last.then_inc(S["turned"], 1)
                        if s.exists():
                            half_xo(s, 1).then_inc(S["o_psum"], 1)
                        if t.exists():
                            pe.wait_ge(S["h3T_done"], t.v + 1)
                            need(pe, S["lg_done"], 2 * t.v)
                            for k in range(KD):
                                last = pe.matmul(psr[:, 0:NG + NE], h3T[:, k, :], wr[:, k, :], start=(k == 0), stop=(k == KD - 1))
                            last.then_inc(S["r_psum"], 1)
                        t = s.at(-2)
                        if t.exists():
                            pe.wait_ge(S["picked"], t.v + 1)
                            need(pe, S["total_done"], t.v)
                            need(pe, S["rk"], t.v)
                            pe.matmul(psk[:, 0:NE], lower[:], picked[t.par][:], start=True, stop=False)
                            pe.matmul(psk[:, 0:NE], ones[:], total[:], start=False, stop=True).then_inc(S["rank_psum"], 1)
                    steps(pe, step, 4, 6, NT + 2)
        NB = NBMAX + 4
        slot_of = sbe("slot_of_block", [1, NB], I32)
        expert_of = sbe("expert_of_block", [1, NB], I32)
        ends = sbe("block_ends", [1, NE], I32)
        starts1 = sbe("block_starts1", [1, NE], I32)
        slot_base = sbe("slot_base", [1, NE + 1], I32)
        with one_stage() as st:
            sb, pb, sem = alloc(st)
            cnt = sb("p_cnt", [1, NE])
            over = sb("p_over", [1, NE, NT])
            limits = sb("p_limits", [1, NT])
            nblk = sb("p_nblk", [1, NE])
            end = sb("p_end", [1, NE])
            zero = sb("p_zero", [1, NE])
            bidx = sb("p_bidx", [1, NB])
            past = sb("p_past", [1, NB, NE])
            pastn = sb("p_pastn", [1, NB, NE])
            eb = sb("p_eb", [1, NB])
            sbk2 = sb("p_sb", [1, NB])
            tmp = sb("p_tmp", [1, NB])
            sf = sb("p_sf", [1, NE])
            psc = pb("p_psc", [P, 512])
            counted = sem("p_counted")
            link = sem("p_link")
            setup = sem("p_setup")
            with nc.Block() as block:
                @block.tensor
                def _(pe):
                    pe.matmul(psc[:, 0:NE], ones[:], total[:], start=True, stop=True).then_inc(counted, 1)

                @block.gpsimd
                def _(pool):
                    pool.iota(limits[:], [[P, NT]], base=0, channel_multiplier=0, allow_small_or_imprecise_dtypes=True).then_inc(setup, 1)
                    pool.iota(bidx[:], [[1, NB]], base=0, channel_multiplier=0, allow_small_or_imprecise_dtypes=True).then_inc(setup, 1)
                    pool.memset(zero[:], 0.0).then_inc(setup, 1)
                    pool.iota(slot_base[:], [[0, (NE + 1) // SLOTS], [EXPERT_COLS, SLOTS]], base=0, channel_multiplier=0).then_inc(setup, 1)

                @block.vector
                def _(dve):
                    n = [0]

                    def then(ins):
                        n[0] += 1
                        ins.then_inc(link, 1)
                        dve.wait_ge(link, n[0])
                    dve.wait_ge(setup, 4)
                    dve.wait_ge(counted, 1)
                    then(dve.tensor_copy(cnt[:], psc[0:1, 0:NE]))
                    then(dve.tensor_tensor(over[:], cnt[:].unsqueeze(2).to_broadcast([1, NE, NT]),
                                           limits[:].unsqueeze(1).to_broadcast([1, NE, NT]), ALU.is_gt))
                    then(dve.tensor_reduce(nblk[:], over[:], X, ALU.add))
                    then(dve.tensor_tensor_scan(end[:], nblk[:], zero[:], 0.0, ALU.add, ALU.add))
                    then(dve.tensor_copy(ends[:], end[:]))
                    then(dve.tensor_tensor(sf[:], end[:], nblk[:], ALU.subtract))
                    then(dve.tensor_scalar(sf[:], sf[:], 1.0, None, ALU.add))
                    then(dve.tensor_copy(starts1[:], sf[:]))
                    then(dve.tensor_tensor(past[:], end[:].unsqueeze(1).to_broadcast([1, NB, NE]),
                                           bidx[:].unsqueeze(2).to_broadcast([1, NB, NE]), ALU.is_le))
                    then(dve.tensor_reduce(eb[:], past[:], X, ALU.add))
                    then(dve.tensor_tensor(pastn[:], past[:], nblk[:].unsqueeze(1).to_broadcast([1, NB, NE]), ALU.mult))
                    then(dve.tensor_reduce(sbk2[:], pastn[:], X, ALU.add))
                    then(dve.tensor_tensor(tmp[:], bidx[:], sbk2[:], ALU.subtract))
                    then(dve.tensor_scalar(tmp[:], tmp[:], float(P), None, ALU.mult))
                    then(dve.scalar_tensor_tensor(out=tmp[:], in0=eb[:], scalar=float(CAP), in1=tmp[:], op0=ALU.mult, op1=ALU.add))
                    then(dve.tensor_scalar(tmp[:], tmp[:], float(NE * CAP - P), None, ALU.min))
                    then(dve.tensor_copy(slot_of[:], tmp[:]))
                    then(dve.tensor_scalar(eb[:], eb[:], float(NE - 1), None, ALU.min))
                    then(dve.tensor_copy(expert_of[:], eb[:]))
        with one_stage() as st:
            sb, pb, sem = alloc(st)
            pair = [sb(f"e_pair{i}", [P, 1], I32) for i in range(2)]
            spair = [sb(f"e_spair{i}", [P, 1], I32) for i in range(2)]
            token = [sb(f"e_token{i}", [P, 1], I32) for i in range(2)]
            xg = [sb(f"e_xg{i}", [P, D]) for i in range(2)]
            xT = [sb(f"e_xT{i}", [P, KD, P]) for i in range(2)]
            sg = sb("e_sg", [P, DE])
            hb = sb("e_hb", [P, DE])
            hT = sb("e_hT", [P, KE, P])
            yb = [sb(f"e_y{i}", [P, D]) for i in range(2)]
            psx = pb("e_psx", [P, KD, P])
            psg = pb("e_psg", [P, DE])
            psu = pb("e_psu", [P, DE])
            psh = pb("e_psh", [P, KE, P])
            psy = pb("e_psy", [P, D])
            names = "token_done x_turned xT_done gate_psum up_psum silu_done h_done h_turned hT_done y_psum y_done blocks_left".split()
            S = {n: sem("e_" + n) for n in names}
            pair_here = [sem(f"e_pair_here{i}") for i in range(2)]
            spair_here = [sem(f"e_spair_here{i}") for i in range(2)]
            x_here = [sem(f"e_x_here{i}") for i in range(2)]
            y_out = [sem(f"e_y_out{i}") for i in range(2)]

            def count_blocks(eng):
                return eng.value_load(ends[0:1, NE - 1:NE], min_val=PAIRS // P, max_val=NBMAX)

            def block_steps(eng, nb, parts):
                def step(b):
                    for k, work in parts:
                        t = b.at(k)
                        if isinstance(t.v, int):
                            if 0 <= t.v < PAIRS // P:
                                work(t)
                                continue
                            if t.v < 0:
                                continue
                        with eng.If(t.v < nb):
                            work(t)
                steps(eng, step, 4, (NBMAX - 3) // 2, NBMAX + 1)

            with nc.Block() as block:
                @block.sync
                def _(sp):
                    for i in range(2):
                        sp.wait_ge(x_here[i], 16)
                    load_expert(sp, 2, 0, 0)

                    def load(e, half, par, slot):
                        first = sp.value_load(starts1[0:1, bass.ds(e - 2, 1)], min_val=1, max_val=NBMAX + 1)
                        sp.wait_ge(S["blocks_left"], first)
                        sp.wait_ge(expert_here[par], 48 * half)
                        load_expert(sp, e, slot, par)
                    with sp.Fori(0, (NE - 3) // 6) as g:
                        for u in range(6):
                            load(6 * g + (3 + u), 3 * g + (3 + u) // 2, (1 + u) % 2, (1 + u) % 3)
                    for e in range(3 + (NE - 3) // 6 * 6, NE):
                        load(e, e // 2, e % 2, (e + 1) % 3)

                @block.gpsimd
                def _(pool):
                    nb = count_blocks(pool)

                    def pairs_of(t):
                        base = pool.value_load(slot_of[0:1, bass.ds(t.v, 1)], min_val=0, max_val=NE * CAP - P)
                        return table_d[bass.ds(base, P), :]

                    def fetch(t):
                        src = pairs_of(t)
                        need(pool, S["token_done"], t.v - 1)
                        pool.dma_start(pair[t.par][:], src).then_inc(pair_here[t.par], 16)

                    def fetch_again(t):
                        src = pairs_of(t)
                        need(pool, y_out[t.par], 16 * t.half)
                        pool.dma_start(spair[t.par][:], src).then_inc(spair_here[t.par], 16)

                    def gather(t):
                        pool.wait_ge(S["token_done"], t.v + 1)
                        need(pool, S["x_turned"], t.v - 1)
                        settle(pool)
                        pool.indirect_dma_start(out=xg[t.par][:], out_offset=None, in_=h3_d,
                                                in_offset=bass.IndirectOffsetOnAxis(ap=token[t.par][:], axis=0)).then_inc(x_here[t.par], 16)

                    def scatter(t):
                        pool.wait_ge(S["y_done"], 2 * t.v + 2)
                        pool.wait_ge(spair_here[t.par], 16 * (t.half + 1))
                        need(pool, y_out[1 - t.par], 16 * (t.half + t.par))
                        settle(pool)
                        pool.indirect_dma_start(out=y_d, out_offset=bass.IndirectOffsetOnAxis(ap=spair[t.par][:], axis=0),
                                                in_=yb[t.par][:], in_offset=None).then_inc(y_out[t.par], 16)
                    fetch(fixed(0))
                    fetch(fixed(1))
                    gather(fixed(0))
                    gather(fixed(1))
                    fetch(fixed(2))
                    block_steps(pool, nb, [(2, gather), (3, fetch), (0, fetch_again), (-1, scatter)])
                    for i in range(2):
                        pool.wait_ge(y_out[i], 16 * ((nb + (1 - i)) // 2))

                @block.scalar
                def _(act):
                    nb = count_blocks(act)

                    def silu(t):
                        act.wait_ge(S["gate_psum"], t.v + 1)
                        need(act, S["h_done"], t.v)
                        act.activation(sg[:], psg[:], ACT.Silu).then_inc(S["silu_done"], 1)

                    def hT_out(t):
                        act.wait_ge(S["h_turned"], t.v + 1)
                        act.wait_ge(S["blocks_left"], t.v + 1)
                        act.activation(hT[:], psh[:], ACT.Copy).then_inc(S["hT_done"], 1)

                    def xT_out(t):
                        act.wait_ge(S["x_turned"], t.v + 1)
                        need(act, S["up_psum"], t.v - 1)
                        act.activation(xT[t.par][:, 0:4, :], psx[:, 0:4, :], ACT.Copy).then_inc(S["xT_done"], 1)

                    def y_evac(t):
                        act.wait_ge(S["y_psum"], t.v + 1)
                        need(act, y_out[t.par], 16 * t.half)
                        act.activation(yb[t.par][:, 0:512], psy[:, 0:512], ACT.Copy).then_inc(S["y_done"], 1)
                    xT_out(fixed(0))
                    block_steps(act, nb, [(-1, hT_out), (0, silu), (1, xT_out), (-1, y_evac)])

                @block.vector
                def _(dve):
                    nb = count_blocks(dve)

                    def tokens(t):
                        dve.wait_ge(pair_here[t.par], 16 * (t.half + 1))
                        need(dve, x_here[t.par], 16 * t.half)
                        dve.tensor_scalar(token[t.par][:], pair[t.par][:], 1, None, ALU.arith_shift_right).then_inc(S["token_done"], 1)

                    def xT_out(t):
                        dve.wait_ge(S["x_turned"], t.v + 1)
                        need(dve, S["up_psum"], t.v - 1)
                        dve.tensor_copy(xT[t.par][:, 4:8, :], psx[:, 4:8, :]).then_inc(S["xT_done"], 1)

                    def hidden(t):
                        dve.wait_ge(S["silu_done"], t.v + 1)
                        dve.wait_ge(S["up_psum"], t.v + 1)
                        need(dve, S["h_turned"], t.v)
                        dve.tensor_tensor(hb[:], psu[:], sg[:], ALU.mult).then_inc(S["h_done"], 1)

                    def y_evac(t):
                        dve.wait_ge(S["blocks_left"], t.v + 2)
                        need(dve, y_out[t.par], 16 * t.half)
                        dve.tensor_copy(yb[t.par][:, 512:1024], psy[:, 512:1024]).then_inc(S["y_done"], 1)
                    tokens(fixed(0))
                    tokens(fixed(1))
                    xT_out(fixed(0))
                    block_steps(dve, nb, [(2, tokens), (0, hidden), (1, xT_out), (-1, y_evac)])

                @block.tensor
                def _(pe):
                    nb = count_blocks(pe)
                    pe.sem_inc(S["blocks_left"], 1)

                    def turn_x(t):
                        pe.wait_ge(x_here[t.par], 16 * (t.half + 1))
                        need(pe, S["xT_done"], 2 * t.v)
                        for k in range(KD):
                            last = pe.transpose(psx[:, k, :], xg[t.par][:, P * k:P * k + P], ident[:])
                        last.then_inc(S["x_turned"], 1)

                    def weights(t):
                        e = pe.value_load(expert_of[0:1, bass.ds(t.v, 1)], min_val=0, max_val=NE - 1)
                        return e, pe.value_load(slot_base[0:1, bass.ds(e + 1, 1)], min_val=0, max_val=(SLOTS - 1) * EXPERT_COLS)

                    def gate_up(t):
                        e, base = weights(t)
                        for i in range(2):
                            with pe.If((e % 2) == i):
                                pe.wait_ge(expert_here[i], 48 * (e // 2 + 1))
                                pe.nop()
                        pe.wait_ge(S["xT_done"], 2 * t.v + 2)
                        need(pe, S["silu_done"], t.v)
                        for k in range(KD):
                            last = pe.matmul(psg[:], xT[t.par][:, k, :], W[:, bass.ds(base + 512 * k, 512)], start=(k == 0), stop=(k == KD - 1))
                        last.then_inc(S["gate_psum"], 1)
                        need(pe, S["h_done"], t.v)
                        for k in range(KD):
                            last = pe.matmul(psu[:], xT[t.par][:, k, :], W[:, bass.ds(base + 4096 + 512 * k, 512)], start=(k == 0), stop=(k == KD - 1))
                        last.then_inc(S["up_psum"], 1)

                    def turn_h(t):
                        pe.wait_ge(S["h_done"], t.v + 1)
                        need(pe, S["hT_done"], t.v)
                        for k in range(KE):
                            last = pe.transpose(psh[:, k, :], hb[:, P * k:P * k + P], ident[:])
                        last.then_inc(S["h_turned"], 1)

                    def down(t):
                        e, base = weights(t)
                        pe.wait_ge(S["hT_done"], t.v + 1)
                        need(pe, S["y_done"], 2 * t.v)
                        for n in range(2):
                            for k in range(KE):
                                last = pe.matmul(psy[:, 512 * n:512 * n + 512], hT[:, k, :],
                                                 W[:, bass.ds(base + 8192 + 1024 * k + 512 * n, 512)], start=(k == 0), stop=(k == KE - 1))
                            last.then_inc(S["blocks_left" if n else "y_psum"], 1)
                    turn_x(fixed(0))
                    block_steps(pe, nb, [(-1, turn_h), (0, gate_up), (1, turn_x), (-1, down)])
        with one_stage() as st:
            sb, pb, sem = alloc(st)
            x2 = [sb(f"f_x2{i}", [P, D]) for i in range(2)]
            y = [sb(f"f_y{i}", [P, 2, D]) for i in range(2)]
            acc = [sb(f"f_acc{i}", [P, D]) for i in range(2)]
            out = [sb(f"f_out{i}", [P, D]) for i in range(2)]
            gl = sb("f_gfinal", [P, D])
            junk = sb("f_junk", [P, D])
            ss = sb("f_ss", [P, 2])
            rs = sb("f_rs", [P, 4])
            S = {n: sem("f_" + n) for n in "gl_here first second squares eps rstd out_done".split()}
            x2_here = [sem(f"f_x2_here{i}") for i in range(2)]
            y_here = [sem(f"f_y_here{i}") for i in range(2)]
            out_sent = [sem(f"f_out_sent{i}") for i in range(2)]
            y_p = O["y_p"].rearrange("b (t p) d -> (b t) p d", p=P)
            y_pairs = y_d[0:PAIRS, :].rearrange("(t p k) d -> t p k d", p=P, k=2)
            with nc.Block() as block:
                @block.sync
                def _(sp):
                    def step(s):
                        if s.exists():
                            need(sp, S["second"], s.v - 1)
                            sp.dma_start(x2[s.par][:], row(x2_d, s)).then_inc(x2_here[s.par], 16)
                            sp.dma_start(y[s.par][:], y_pairs[bass.ds(s.v, 1), :, :, :].rearrange("a p k d -> (a p) k d")).then_inc(y_here[s.par], 16)
                    steps(sp, step, 4, 6, NT)

                @block.gpsimd
                def _(pool):
                    def step(t):
                        pool.wait_ge(S["squares"], t.v + 1)
                        need(pool, S["out_done"], t.v)
                        settle(pool)
                        pool.tensor_scalar(rs[:, 0:1], ss[:, 0:1], EPS, None, ALU.add).then_inc(S["eps"], 1)
                        pool.wait_ge(S["eps"], t.v + 1)
                        pool.tensor_tensor(rs[:, 1:2], rs[:, 0:1], mhalf[:], ALU.pow).then_inc(S["rstd"], 1)
                    steps(pool, step, 4, 6, NT)

                @block.scalar
                def _(act):
                    act.dma_start(gl[:], I["g_final"].rearrange("(a d) -> a d", a=1).partition_broadcast(P).rearrange("p a d -> p (a d)")).then_inc(S["gl_here"], 16)

                    def store(t):
                        act.wait_ge(S["out_done"], t.v + 1)
                        dst = O["y_s"].rearrange("b t d -> (b t) d") if isinstance(t.v, int) and t.v == PT else \
                            y_p[bass.ds(t.v, 1), :, :].rearrange("a p d -> (a p) d")
                        act.dma_start(dst, out[t.par][:]).then_inc(out_sent[t.par], 16)

                    def step(s):
                        if s.exists():
                            act.wait_ge(S["second"], s.v + 1)
                            need(act, S["rstd"], s.v)
                            need(act, S["squares"], s.v)
                            act.activation(junk[:], acc[s.par][:], ACT.Square, scale=1 / 32, accum_out=ss[:, 0:1]).then_inc(S["squares"], 1)
                        if s.at(-1).exists():
                            store(s.at(-1))
                    steps(act, step, 4, 6, NT + 1)
                    act.wait_ge(out_sent[0], 16 * 9)
                    act.wait_ge(out_sent[1], 16 * 8)

                @block.vector
                def _(dve):
                    dve.wait_ge(S["gl_here"], 16)

                    def step(s):
                        g = gates[:, bass.ds(s.v, 1), :].rearrange("p a k -> p (a k)") if s.exists() else None
                        if s.exists():
                            dve.wait_ge(x2_here[s.par], 16 * (s.half + 1))
                            dve.wait_ge(y_here[s.par], 16 * (s.half + 1))
                            need(dve, S["out_done"], s.v - 1)
                            dve.scalar_tensor_tensor(out=acc[s.par][:], in0=y[s.par][:, 0, :], scalar=g[:, 0:1], in1=x2[s.par][:],
                                                     op0=ALU.mult, op1=ALU.add).then_inc(S["first"], 1)
                            dve.wait_ge(S["first"], s.v + 1)
                            dve.scalar_tensor_tensor(out=acc[s.par][:], in0=y[s.par][:, 1, :], scalar=g[:, 1:2], in1=acc[s.par][:],
                                                     op0=ALU.mult, op1=ALU.add).then_inc(S["second"], 1)
                        t = s.at(-1)
                        if t.exists():
                            dve.wait_ge(S["rstd"], t.v + 1)
                            need(dve, out_sent[t.par], 16 * t.half)
                            dve.scalar_tensor_tensor(out=out[t.par][:], in0=acc[t.par][:], scalar=rs[:, 1:2], in1=gl[:],
                                                     op0=ALU.mult, op1=ALU.mult).then_inc(S["out_done"], 1)
                    steps(dve, step, 4, 6, NT + 1)
        e_stack.close()


_INS = ["x_prompt", "x_sample", "mem_prompt", "state_conv", "cache_mem_k", "cache_mem_v", "g_mix", "w_in", "conv_w", "conv_b",
        "ln_conv_g", "ln_conv_b", "ln_v_g", "ln_v_b", "w_sg", "b_sg", "w_out", "g_mem", "w_mk", "w_mv", "g_xattn", "w_xq",
        "w_xo", "g_ffn", "w_router_group", "b_router_group", "w_router_expert", "b_router_expert", "w_expert_gate",
        "w_expert_up", "w_expert_down", "g_final"]
_OUTS = {"y_p": (1, 2048, D), "y_s": (SEQS, SLEN, D), "state_p": (HIST, DC), "state_s": (SEQS, HIST, DC),
         "k": (NMEM, D), "v": (NMEM, D), "sgv": (P, DC)}


def kernel(**inputs):
    import concourse.bacc as bacc
    from concourse.bass_utils import run_bass_kernel_spmd

    nc = bacc.Bacc("TRN2", target_bir_lowering=False, num_devices=1)
    arrays, I, O = {}, {}, {}
    for name in _INS:
        a = np.ascontiguousarray(inputs[name])
        arrays[f"in_{name}"] = a
        I[name] = nc.dram_tensor(f"in_{name}", a.shape, mybir.dt.from_np(a.dtype), kind="ExternalInput").ap()
    for name, shape in _OUTS.items():
        O[name] = nc.dram_tensor(f"out_{name}", shape, F32, kind="ExternalOutput").ap()
    build(nc, I, O)
    r = run_bass_kernel_spmd(nc, [arrays], core_ids=[0]).results[0]
    return (r["out_y_p"], r["out_y_s"], r["out_state_p"].reshape(1, 1, HIST, DC), r["out_state_s"].reshape(1, SEQS, HIST, DC),
            r["out_k"].reshape(1, 1, NMEM, HEADS, HD), r["out_v"].reshape(1, 1, NMEM, HEADS, HD),
            r["out_sgv"].reshape(1, SEQS, SLEN, DC))
```
